# Optimizing a Trainium2 kernel written in Bass

```python
import jax
import jax.numpy as jnp
from jax import lax
import numpy as np

D_MODEL = 1024
BATCH = 1
SEQ = 256
DEPTH = 1

LRU_HEADS = 8
LRU_WIDTH = D_MODEL // 2
LRU_HEAD_DIM = LRU_WIDTH // LRU_HEADS
LRU_CONV = 4
LRU_C = 8.0
ATTN_HEADS = 8
ATTN_WIDTH = D_MODEL // 2
HEAD_DIM = ATTN_WIDTH // ATTN_HEADS
MIX_WIDTH = LRU_WIDTH + ATTN_WIDTH
IN_WIDTH = 2 * LRU_WIDTH + 3 * ATTN_WIDTH
MOBA_BLOCK = 256
MOBA_TOPK = 3
Q_CHUNK = 32
D_FF = 2816
FFN_CONV = 3
EPS = 1e-6

kernel_name = 'hybrid_rglru_moba_convffn'

def rms_norm(x, g):
    xf = x.astype(jnp.float32)
    y = xf * lax.rsqrt(jnp.mean(xf * xf, axis=-1, keepdims=True) + EPS)
    return (y * g.astype(jnp.float32)).astype(x.dtype)

def causal_depthwise_conv(x, w, b):
    width, ch = w.shape
    y = lax.conv_general_dilated(
        x, w[:, None, :].astype(x.dtype), window_strides=(1,),
        padding=[(width - 1, 0)], dimension_numbers=('NWC', 'WIO', 'NWC'),
        feature_group_count=ch)
    return y + b.astype(x.dtype)

def rg_lru(xr, w_a, b_a, w_i, b_i, lam):
    bsz, seq, _ = xr.shape
    xf = xr.astype(jnp.float32)
    xh = xf.reshape(bsz, seq, LRU_HEADS, LRU_HEAD_DIM)
    r = jax.nn.sigmoid(jnp.einsum('bshi,hij->bshj', xh, w_a.astype(jnp.float32)).reshape(bsz, seq, LRU_WIDTH) + b_a.astype(jnp.float32))
    i = jax.nn.sigmoid(jnp.einsum('bshi,hij->bshj', xh, w_i.astype(jnp.float32)).reshape(bsz, seq, LRU_WIDTH) + b_i.astype(jnp.float32))
    log_a = -LRU_C * r * jax.nn.softplus(-lam.astype(jnp.float32))
    a = jnp.exp(log_a)
    u = jnp.sqrt(-jnp.expm1(2.0 * log_a)) * (i * xf)

    def combine(left, right):
        a_l, h_l = left
        a_r, h_r = right
        return a_l * a_r, a_r * h_l + h_r

    _, h = lax.associative_scan(combine, (a, u), axis=1)
    return h

def moba_attention(q, k, v):
    bsz, seq, heads, dh = q.shape
    n_blocks = -(-seq // MOBA_BLOCK)
    s_pad = n_blocks * MOBA_BLOCK
    k_sel = max(1, min(MOBA_TOPK, n_blocks - 1))
    scale = dh ** -0.5
    neg = jnp.finfo(jnp.float32).min
    slopes = jnp.exp2(-8.0 * jnp.arange(1, heads + 1, dtype=jnp.float32) / heads)
    qh = q.astype(jnp.float32).transpose(0, 2, 1, 3)
    pad = ((0, 0), (0, 0), (0, s_pad - seq), (0, 0))
    kb = jnp.pad(k.astype(jnp.float32).transpose(0, 2, 1, 3), pad).reshape(bsz, heads, n_blocks, MOBA_BLOCK, dh)
    vb = jnp.pad(v.astype(jnp.float32).transpose(0, 2, 1, 3), pad).reshape(bsz, heads, n_blocks, MOBA_BLOCK, dh)
    k_mean = kb.mean(axis=3)
    q_blk = jnp.arange(seq) // MOBA_BLOCK
    fully_past = jnp.arange(n_blocks)[None, :] < q_blk[:, None]
    gate = jnp.where(fully_past, jnp.einsum('bhsd,bhnd->bhsn', qh, k_mean), neg)
    _, sel = lax.top_k(gate, k_sel)
    sel_ok = sel < q_blk[:, None]
    gather_blocks = jax.vmap(jax.vmap(lambda blocks, ids: blocks[ids]))
    offs = jnp.arange(MOBA_BLOCK)

    def query_chunk(c):
        start = c * Q_CHUNK
        q_c = lax.dynamic_slice_in_dim(qh, start, Q_CHUNK, axis=2)
        sel_c = lax.dynamic_slice_in_dim(sel, start, Q_CHUNK, axis=2)
        ok_c = lax.dynamic_slice_in_dim(sel_ok, start, Q_CHUNK, axis=2)
        q_pos = start + jnp.arange(Q_CHUNK)
        k_g = gather_blocks(kb, sel_c)
        v_g = gather_blocks(vb, sel_c)
        dist_g = (q_pos[:, None, None] - (sel_c[..., None] * MOBA_BLOCK + offs)).astype(jnp.float32)
        s_g = jnp.einsum('bhqd,bhqnkd->bhqnk', q_c, k_g) * scale - slopes[:, None, None, None] * dist_g
        s_g = jnp.where(ok_c[..., None], s_g, neg)
        own = start // MOBA_BLOCK
        k_o = lax.dynamic_index_in_dim(kb, own, axis=2, keepdims=False)
        v_o = lax.dynamic_index_in_dim(vb, own, axis=2, keepdims=False)
        dist_o = q_pos[:, None] - (own * MOBA_BLOCK + offs)[None, :]
        s_o = jnp.einsum('bhqd,bhkd->bhqk', q_c, k_o) * scale - slopes[:, None, None] * dist_o.astype(jnp.float32)
        s_o = jnp.where(dist_o >= 0, s_o, neg)
        logits = jnp.concatenate([s_g.reshape(bsz, heads, Q_CHUNK, k_sel * MOBA_BLOCK), s_o], axis=-1)
        p = jax.nn.softmax(logits, axis=-1)
        p_g = p[..., :k_sel * MOBA_BLOCK].reshape(bsz, heads, Q_CHUNK, k_sel, MOBA_BLOCK)
        p_o = p[..., k_sel * MOBA_BLOCK:]
        return jnp.einsum('bhqnk,bhqnkd->bhqd', p_g, v_g) + jnp.einsum('bhqk,bhkd->bhqd', p_o, v_o)

    out = lax.map(query_chunk, jnp.arange(seq // Q_CHUNK))
    return out.transpose(1, 0, 3, 2, 4).reshape(bsz, seq, heads * dh)

def setup_inputs(seed: int = 0) -> dict:
    key = jax.random.key(seed)
    ks = jax.random.split(key, 24)
    f32 = jnp.float32

    def nrm(k, shape, scale):
        return jax.random.normal(k, shape, f32) * scale

    def gain(k, n):
        return 1.0 + 0.05 * jax.random.normal(k, (DEPTH, n), f32)

    u = jax.random.uniform(ks[11], (DEPTH, LRU_WIDTH), f32, 0.9, 0.999)
    a_base = u ** (1.0 / LRU_C)
    return {
        'x': nrm(ks[0], (BATCH, SEQ, D_MODEL), 1.0),
        'mix_norm_g': gain(ks[1], D_MODEL),
        'w_in': nrm(ks[2], (DEPTH, D_MODEL, IN_WIDTH), D_MODEL ** -0.5),
        'lru_conv_w': nrm(ks[3], (DEPTH, LRU_CONV, LRU_WIDTH), LRU_CONV ** -0.5),
        'lru_conv_b': nrm(ks[4], (DEPTH, LRU_WIDTH), 0.02),
        'lru_w_a': nrm(ks[5], (DEPTH, LRU_HEADS, LRU_HEAD_DIM, LRU_HEAD_DIM), LRU_HEAD_DIM ** -0.5),
        'lru_b_a': nrm(ks[6], (DEPTH, LRU_WIDTH), 0.02),
        'lru_w_i': nrm(ks[7], (DEPTH, LRU_HEADS, LRU_HEAD_DIM, LRU_HEAD_DIM), LRU_HEAD_DIM ** -0.5),
        'lru_b_i': nrm(ks[8], (DEPTH, LRU_WIDTH), 0.02),
        'lru_lambda': jnp.log(a_base) - jnp.log1p(-a_base),
        'q_norm_g': gain(ks[9], HEAD_DIM),
        'k_norm_g': gain(ks[10], HEAD_DIM),
        'lru_out_g': gain(ks[12], LRU_WIDTH),
        'attn_out_g': gain(ks[13], ATTN_WIDTH),
        'w_out': nrm(ks[14], (DEPTH, MIX_WIDTH, D_MODEL), MIX_WIDTH ** -0.5),
        'ffn_norm_g': gain(ks[15], D_MODEL),
        'w_up': nrm(ks[16], (DEPTH, D_MODEL, 2 * D_FF), D_MODEL ** -0.5),
        'ffn_conv_w': nrm(ks[17], (DEPTH, FFN_CONV, 2 * D_FF), FFN_CONV ** -0.5),
        'ffn_conv_b': nrm(ks[18], (DEPTH, 2 * D_FF), 0.02),
        'w_down': nrm(ks[19], (DEPTH, D_FF, D_MODEL), D_FF ** -0.5),
    }

def reference(x, mix_norm_g, w_in, lru_conv_w, lru_conv_b, lru_w_a, lru_b_a, lru_w_i, lru_b_i, lru_lambda, q_norm_g, k_norm_g, lru_out_g, attn_out_g, w_out, ffn_norm_g, w_up, ffn_conv_w, ffn_conv_b, w_down):
    bsz, seq, _ = x.shape
    splits = [LRU_WIDTH, 2 * LRU_WIDTH, 2 * LRU_WIDTH + ATTN_WIDTH, 2 * LRU_WIDTH + 2 * ATTN_WIDTH]
    for layer in range(DEPTH):
        h = rms_norm(x, mix_norm_g[layer])
        proj = h @ w_in[layer]
        xr, yg, q, k, v = jnp.split(proj, splits, axis=-1)
        xr = causal_depthwise_conv(xr, lru_conv_w[layer], lru_conv_b[layer])
        y_lru = rg_lru(xr, lru_w_a[layer], lru_b_a[layer], lru_w_i[layer], lru_b_i[layer], lru_lambda[layer]) * jax.nn.gelu(yg.astype(jnp.float32))
        q = rms_norm(q.reshape(bsz, seq, ATTN_HEADS, HEAD_DIM), q_norm_g[layer])
        k = rms_norm(k.reshape(bsz, seq, ATTN_HEADS, HEAD_DIM), k_norm_g[layer])
        v = v.reshape(bsz, seq, ATTN_HEADS, HEAD_DIM)
        y_attn = moba_attention(q, k, v)
        mixed = jnp.concatenate([rms_norm(y_lru, lru_out_g[layer]), rms_norm(y_attn, attn_out_g[layer])], axis=-1).astype(x.dtype)
        x = x + mixed @ w_out[layer]
        hf = rms_norm(x, ffn_norm_g[layer])
        up = causal_depthwise_conv(hf @ w_up[layer], ffn_conv_w[layer], ffn_conv_b[layer])
        gate, val = jnp.split(up, 2, axis=-1)
        x = x + (jax.nn.gelu(gate) * val) @ w_down[layer]
    return x


_drawn_inputs = setup_inputs


def setup_inputs(seed=0):
    import zlib

    import numpy as np

    out = dict(_drawn_inputs(seed))
    spreads = {}
    factors = {'lru_b_a': 21.553, 'lru_b_i': 8.0, 'ffn_conv_b': 4.836}
    for name, (base, spread) in spreads.items():
        noise = np.random.default_rng([zlib.crc32(name.encode()), seed]).standard_normal(out[name].shape)
        drawn = base * np.exp(spread * noise) if base else spread * noise
        out[name] = jnp.asarray(drawn.astype(out[name].dtype))
    for name, factor in factors.items():
        out[name] = (out[name] * factor).astype(out[name].dtype)
    return out
```

```python
from contextlib import ExitStack

import concourse.bass as bass
from concourse import mybir

F32 = mybir.dt.float32
F32R = mybir.dt.float32r
ACT = mybir.ActivationFunctionType
ALU = mybir.AluOpType
AX_X = mybir.AxisListType.X

P = 128
D_MODEL = 1024
SEQ = 256
LRU_WIDTH = 512
LRU_HEADS = 8
LRU_HEAD_DIM = LRU_WIDTH // LRU_HEADS
LRU_CONV = 4
LRU_C = 8.0
ATTN_WIDTH = 512
HEADS = 8
HEAD_DIM = ATTN_WIDTH // HEADS
D_FF = 2816
FFN_CONV = 3
EPS = 1e-6

KC = D_MODEL // P
TT = SEQ // P
LC = LRU_WIDTH // P
STEPS = D_FF // P
UNIT = 1024
RAW = 6
RING = 6
MASKED = -3.0e38
KEYS = [P, 2 * P]
KEY_AT = [0, P]
SCORES = sum(KEYS)

U_X, U_Q, U_K, U_Y, U_V, U_O = 0, 4, 8, 12, 16, 20
U_FFN = 28
LOOP_STEPS = 4
LOOPS = (STEPS - 2) // LOOP_STEPS
LOOP_UNITS = 3 * LOOP_STEPS
U_LOOP = U_FFN + 5
U_LAST = U_LOOP + LOOPS * LOOP_UNITS
assert (STEPS - 2) % LOOP_STEPS == 0 and LOOP_UNITS % RING == 0

MIX_G, CONV_W, CONV_B, B_A, B_I, LAMBDA = 0, 8, 24, 28, 32, 36
LRU_G, ATTN_G, FFN_G, Q_G, K_G = 40, 44, 48, 56, 57
N_PAR = 58
N_FPAR = 2 * 2 * STEPS


def build_layer(nc, x, mix_norm_g, w_in, lru_conv_w, lru_conv_b, lru_w_a, lru_b_a, lru_w_i, lru_b_i,
                lru_lambda, q_norm_g, k_norm_g, lru_out_g, attn_out_g, w_out, ffn_norm_g, w_up,
                ffn_conv_w, ffn_conv_b, w_down, out):
    with ExitStack() as ctx:
        def sb(name, shape, dt=F32):
            return ctx.enter_context(nc.sbuf_tensor(name, shape, dt))

        def sem(name):
            return ctx.enter_context(nc.semaphore(name))

        bank = [ctx.enter_context(nc.psum_tensor(f"bank{b}", [P, 512], F32)) for b in range(8)]
        raw = [sb(f"raw{r}", [P, 2 * UNIT]) for r in range(RAW)]
        w_hi = [sb(f"w_hi{r}", [P, UNIT], F32R) for r in range(RING)]
        w_lo = [sb(f"w_lo{r}", [P, UNIT], F32R) for r in range(RING)]
        x_tok = sb("x_tok", [P, TT, D_MODEL])
        h_hi = sb("h_hi", [P, KC, SEQ], F32R)
        h_lo = sb("h_lo", [P, KC, SEQ], F32R)
        mix_hi = sb("mix_hi", [P, KC, SEQ], F32R)
        mix_lo = sb("mix_lo", [P, KC, SEQ], F32R)
        xc = sb("xc", [P, LC, SEQ])
        gate_r = sb("gate_r", [P, LC, SEQ])
        gate_i = sb("gate_i", [P, LC, SEQ])
        decay = sb("decay", [P, LC, SEQ])
        tanh_a = sb("tanh_a", [P, LC, SEQ])
        ygate = sb("ygate", [P, LC, SEQ])
        qk_tok = sb("qk_tok", [P, 2 * TT, ATTN_WIDTH])
        q_T = sb("q_T", [P, LC, SEQ])
        k_T = sb("k_T", [P, LC, SEQ])
        v_tok = sb("v_tok", [P, TT, ATTN_WIDTH])
        p_T = sb("p_T", [P, HEADS, SCORES])
        act_hi = sb("act_hi", [P, 2, SEQ], F32R)
        act_lo = sb("act_lo", [P, 2, SEQ], F32R)
        neg_dist = sb("neg_dist", [P, SCORES])
        ident = sb("ident", [P, P])
        ones = sb("ones", [P, P])
        diag = sb("diag", [P, TT, P])
        par = sb("par", [P, N_PAR])
        fpar_a = sb("fpar_a", [P, N_FPAR])
        fpar_b = sb("fpar_b", [P, N_FPAR])
        small = sb("small", [P, 200])
        probs = [qk_tok[:, :, :].rearrange("p a b -> p (a b)")[:, SCORES * j:SCORES * (j + 1)]
                 for j in range(4)]
        conv_g = [xc[:, j, :] for j in range(2)]
        conv_v = [xc[:, 2 + j, :] for j in range(2)]
        gelu_g = [gate_r[:, j, :] for j in range(2)]
        prod = [gate_i[:, j, :] for j in range(2)]
        y_attn = [q_T[:, :, :].rearrange("p c t -> p (c t)")[:, 0:512],
                  q_T[:, :, :].rearrange("p c t -> p (c t)")[:, 512:1024]]
        rows = [p_T[:, 0, 0:P], p_T[:, 0, P:2 * P], p_T[:, 0, 2 * P:3 * P]]
        w_gate = p_T[:, 4:8, :].rearrange("p h s -> p (h s)")[:, 0:2 * LC * P].rearrange(
            "p (g c j) -> p g c j", g=2, c=LC)

        def flat(t):
            return t[:, :, :].rearrange("p c t -> p (c t)")

        sq_tok = flat(p_T)[:, 2560:3072]
        eps = small[:, 0:1]
        x_ss, x_rms, x_rstd = small[:, 2:4], small[:, 4:6], small[:, 6:8]
        lam_u, lam_z, lam_z2, lam_s, log_c = (small[:, 8 + 4 * j:12 + 4 * j] for j in range(5))
        row_sum = small[:, 28:44].rearrange("p (h m) -> p h m", m=TT)
        neg_max = small[:, 44:60].rearrange("p (h m) -> p h m", m=TT)
        row_rec = small[:, 60:76].rearrange("p (h m) -> p h m", m=TT)
        q_scale = small[:, 76:80]
        y_rms, y_rstd = small[:, 80:82], small[:, 82:84]
        a_ss, a_rms, a_rstd = small[:, 84:86], small[:, 86:88], small[:, 88:90]
        f_ss, f_sum, f_rms, f_rstd = small[:, 90:94], small[:, 94:96], small[:, 96:98], small[:, 98:100]
        lam_p = small[:, 100:104]
        qk_ss, qk_rms, qk_rstd = (small[:, 104 + 32 * j:136 + 32 * j].rearrange("p (g h) -> p g h", h=HEADS)
                                  for j in range(3))

        raw_landed = [sem(f"raw_landed{r}") for r in range(RAW)]
        x_landed = [sem(f"x_landed{m}") for m in range(TT)]
        par_landed = sem("par_landed")
        fpar_landed = sem("fpar_landed")
        gates_landed = sem("gates_landed")
        out_stored = sem("out_stored")
        hi_done, lo_done, unit_used = sem("hi_done"), sem("lo_done"), sem("unit_used")
        consts = sem("consts")
        dist_done = sem("dist_done")
        par_T, par_ready = sem("par_T"), sem("par_ready")
        x_sq, x_sq_1 = sem("x_sq"), sem("x_sq_1")
        gates_zero, q_scale_done, f_added = sem("gates_zero"), sem("q_scale_done"), sem("f_added")
        x_rms_done, diag_done = sem("x_rms_done"), sem("diag_done")
        xT, hT_hi, hT_lo = sem("xT"), sem("hT_hi"), sem("hT_lo")
        conv_base, conv_done = sem("conv_base"), sem("conv_done")
        gates_done, gates_read = sem("gates_done"), sem("gates_read")
        lam_exp, log_c_done = sem("lam_exp"), sem("log_c_done")
        decay_done, a2_done, one_m_a2, root_done = sem("decay_done"), sem("a2_done"), sem("one_m_a2"), sem("root_done")
        lru_in, scan_done = sem("lru_in"), sem("scan_done")
        ygate_done, y_done, y_sq = sem("ygate_done"), sem("y_done"), sem("y_sq")
        y_sum, y_rms_done, y_diag, y_bc = sem("y_sum"), sem("y_rms_done"), sem("y_diag"), sem("y_bc")
        y_scaled, mix_ready = sem("y_scaled"), sem("mix_ready")
        qk_sq, qk_sum, qk_rms_done, qk_norm = sem("qk_sq"), sem("qk_sum"), sem("qk_rms_done"), sem("qk_norm")
        qkT, qkT_read = sem("qkT"), sem("qkT_read")
        v_ready = sem("v_ready")
        scores, shifted, probs_done = sem("scores"), sem("shifted"), sem("probs_done")
        pT, pT_read = sem("pT"), sem("pT_read")
        o_done, attn_out, a_sq, a_rms_done, a_diag = sem("o_done"), sem("attn_out"), sem("a_sq"), sem("a_rms_done"), sem("a_diag")
        aT, aT_hi = sem("aT"), sem("aT_hi")
        wout_done, x2_done, f_sq, f_rms_done, f_diag = sem("wout_done"), sem("x2_done"), sem("f_sq"), sem("f_rms_done"), sem("f_diag")
        fT, fT_hi, fT_lo = sem("fT"), sem("fT_hi"), sem("fT_lo")
        up_base, conv_g_done, conv_v_done, gelu_done, act_ready = (
            sem("up_base"), sem("conv_g_done"), sem("conv_v_done"), sem("gelu_done"), sem("act_ready"))
        tap_g, tap_v, prod_done, act_hi_done = sem("tap_g"), sem("tap_v"), sem("prod_done"), sem("act_hi_done")
        chain = sem("chain")
        pool_chain = sem("pool_chain")
        down_done, final = sem("down_done"), sem("final")

        w_in_c = w_in[0].rearrange("(kc p) n -> p kc n", p=P)
        w_out_c = w_out[0].rearrange("(kc p) n -> p kc n", p=P)
        w_up_c = w_up[0].rearrange("(kc p) n -> p kc n", p=P)
        w_down_c = w_down[0].rearrange("(j p) n -> p j n", p=P)

        head_dmas = []
        for part, col in ((U_X, 0), (U_Q, 1024), (U_K, 1536), (U_Y, 512), (U_V, 2048)):
            for half in range(2):
                if part in (U_X, U_Y):
                    head_dmas.append(w_in_c[:, :, col + 256 * half:col + 256 * (half + 1)])
                else:
                    head_dmas.append(w_in_c[:, 4 * half:4 * (half + 1), col:col + 512])
        for j in range(4):
            head_dmas.append(w_out_c[:, 2 * j:2 * j + 2, :])
        N_HEAD = len(head_dmas)

        def part_of(n, half, by_cols):
            buf = raw[n % RAW]
            if by_cols:
                return buf[:, :].rearrange("p (kc n) -> p kc n", kc=KC)[:, :, P * half:P * (half + 1)]
            return buf[:, UNIT * half:UNIT * (half + 1)]

        def head_unit(u):
            by_cols = u < U_Q or U_Y <= u < U_V
            return u // 2, part_of(u // 2, u % 2, by_cols), by_cols

        def ffn_unit(s, kind):
            n, by_cols = N_HEAD + 3 * (s // 2) + "gvd".index(kind), kind != "d"
            return n, part_of(n, s % 2, by_cols), by_cols

        def as_unit(tile, by_cols):
            return tile[:, :].rearrange("p (kc n) -> p kc n", kc=KC) if by_cols else tile[:, :]

        def ffn_units(s):
            if s == 0:
                return [(U_FFN, 0, "g"), (U_FFN + 1, 0, "v")]
            u = U_FFN + 3 * s - 1
            last = [(u + 2, s - 1, "d")]
            return [(u, s, "g"), (u + 1, s, "v")] + last

        def up_bank(s, which):
            return bank[(0, 1, 4, 5)[2 * (s % 2) + which]]

        DOWN = (2, 3, 6, 7)
        O_ACC = (0, 1, 4, 5)
        QK_T = (2, 3, 4, 5)

        def f_at(kc):
            return bank[DOWN[kc // 2]][:, SEQ * (kc % 2):SEQ * (kc % 2 + 1)]

        def slope(h):
            return 2.0 ** (-8.0 * (h + 1) / HEADS)

        def at_pass(it, per, value):
            return value if it is None else it * per + value

        block = ctx.enter_context(nc.Block())

        @block.sync
        def _(sp):
            x_t = x[0].rearrange("(m p) d -> m p d", p=P)
            for m in range(TT):
                sp.dma_start(x_tok[:, m, :], x_t[m]).then_inc(x_landed[m], 16)

            def load(n, src, units_split=None):
                if units_split is not None:
                    sp.wait_ge(lo_done, units_split)
                dst = raw[n % RAW][:, :].rearrange("p (a b) -> p a b", a=src.shape[1])
                sp.dma_start(dst, src).then_inc(raw_landed[n % RAW], 16)

            for n, src in enumerate(head_dmas):
                load(n, src, 2 * (n - RAW) + 2 if n >= RAW else None)
            load(N_HEAD, w_up_c[:, :, 0:2 * P], 2 * (N_HEAD - RAW) + 2)
            load(N_HEAD + 1, w_up_c[:, :, D_FF:D_FF + 2 * P], 2 * (N_HEAD - RAW) + 4)
            load(N_HEAD + 2, w_down_c[:, 0:2, :], 2 * (N_HEAD - RAW) + 6)
            with sp.Fori(0, LOOPS) as it:
                for k in range(LOOP_STEPS // 2):
                    n = N_HEAD + 3 * (1 + k)
                    i = it * (LOOP_STEPS // 2) + (1 + k)
                    split = [U_LOOP - 8 + 6 * k + j for j in (0, 1, 5)]
                    load(n, w_up_c[:, :, bass.ds(i * (2 * P), 2 * P)], it * LOOP_UNITS + split[0])
                    load(n + 1, w_up_c[:, :, bass.ds(i * (2 * P) + D_FF, 2 * P)],
                         it * LOOP_UNITS + split[1])
                    load(n + 2, w_down_c[:, bass.ds(i * 2, 2), :], it * LOOP_UNITS + split[2])
            out_t = out[0].rearrange("(m p) d -> m p d", p=P)
            for m in range(TT):
                for n in range(2):
                    sp.wait_ge(final, 2 * m + n + 1)
                    sp.dma_start(out_t[m][:, 512 * n:512 * (n + 1)],
                                 x_tok[:, m, 512 * n:512 * (n + 1)]).then_inc(out_stored, 16)
            sp.wait_ge(out_stored, 16 * 2 * TT)

        @block.gpsimd
        def _(pool):
            pool.memset(w_gate, 0.0).then_inc(gates_zero, 1)
            pool.memset(ones[:, :], 1.0).then_inc(pool_chain, 1)
            pool.memset(eps, EPS).then_inc(consts, 1)
            pool.wait_ge(pool_chain, 1)
            pool.affine_select(out=ident[:, :], in_=ones[:, :], compare_op=ALU.is_equal, fill=0.0, base=0,
                               pattern=[[-1, P]], channel_multiplier=1).then_inc(consts, 1)
            for m in range(TT):
                view = neg_dist[:, KEY_AT[m]:KEY_AT[m] + KEYS[m]]
                pool.iota(view, pattern=[[1, KEYS[m]]], base=-P * m, channel_multiplier=-1,
                          allow_small_or_imprecise_dtypes=True).then_inc(pool_chain, 1)
                pool.wait_ge(pool_chain, 2 + m)
                pool.affine_select(out=view, in_=view, compare_op=ALU.is_ge, fill=MASKED, base=P * m,
                                   pattern=[[-1, KEYS[m]]], channel_multiplier=1).then_inc(dist_done, 1)
            for h in range(HEADS):
                half = HEAD_DIM * (h % 2)
                pool.wait_ge(dist_done, TT + h)
                pool.memset(q_scale[half:half + HEAD_DIM, h // 2:h // 2 + 1],
                            HEAD_DIM ** -0.5 / slope(h)).then_inc(dist_done, 1)

        @block.scalar
        def _(act):
            def row_load(dst, src, done):
                act.dma_start(dst, src).then_inc(done, 16)

            def rows_of(t, n):
                return t[0].rearrange("(c p) -> c p", p=P)[0:n]

            row_load(rows[0][MIX_G:MIX_G + KC], rows_of(mix_norm_g, KC), par_landed)
            row_load(rows[0][CONV_W:CONV_W + LRU_CONV * LC],
                     lru_conv_w[0].rearrange("t (c p) -> (t c) p", p=P), par_landed)
            for at, t in ((CONV_B, lru_conv_b), (B_A, lru_b_a), (B_I, lru_b_i), (LAMBDA, lru_lambda),
                          (LRU_G, lru_out_g), (ATTN_G, attn_out_g)):
                row_load(rows[0][at:at + LC], rows_of(t, LC), par_landed)
            row_load(rows[0][FFN_G:FFN_G + KC], rows_of(ffn_norm_g, KC), par_landed)
            for at, t in ((Q_G, q_norm_g), (K_G, k_norm_g)):
                for e in range(2):
                    row_load(rows[0][at:at + 1, HEAD_DIM * e:HEAD_DIM * (e + 1)], t, par_landed)
            fw = ffn_conv_w[0].rearrange("t (c p) -> (t c) p", p=P)
            row_load(rows[1][0:N_FPAR], fw[0:N_FPAR], fpar_landed)
            row_load(rows[2][0:2 * STEPS], fw[N_FPAR:], fpar_landed)
            row_load(rows[2][2 * STEPS:N_FPAR], rows_of(ffn_conv_b, 2 * STEPS), fpar_landed)
            act.wait_ge(gates_zero, 1)
            for g, t in enumerate((lru_w_a, lru_w_i)):
                for e in range(2):
                    half = slice(LRU_HEAD_DIM * e, LRU_HEAD_DIM * (e + 1))
                    row_load(w_gate[half, g, :, half],
                             t[0].rearrange("(c e) i j -> e i c j", e=2)[e], gates_landed)

            def hi(u, raw_unit, it=None):
                n, src, by_cols = raw_unit
                act.wait_ge(raw_landed[n % RAW], at_pass(it, 16, 16 * (n // RAW + 1)))
                if u >= RING:
                    act.wait_ge(unit_used, at_pass(it, LOOP_UNITS, u - RING + 1))
                act.activation(as_unit(w_hi[u % RING], by_cols), src, ACT.Copy).then_inc(hi_done, 1)

            def his(*units):
                for u in units:
                    hi(u, head_unit(u))

            act.wait_ge(x_landed[0], 16)
            act.activation(flat(ygate), x_tok[:, 0, :], ACT.Square, accum_out=x_ss[:, 0:1]).then_inc(x_sq, 1)
            act.wait_ge(consts, 1)
            for m in range(TT):
                if m == 0:
                    act.wait_ge(x_sq, 1)
                else:
                    act.wait_ge(x_sq_1, 1)
                act.activation(x_rms[:, m:m + 1], x_ss[:, m:m + 1], ACT.Sqrt, bias=eps,
                               scale=1.0 / D_MODEL).then_inc(x_rms_done, 1)
            his(0)
            act.wait_ge(par_ready, 1)
            for kc in range(KC):
                act.wait_ge(xT, kc + 1)
                act.activation(h_hi[:, kc, :], bank[kc][:, 0:SEQ], ACT.Copy,
                               scale=par[:, MIX_G + kc:MIX_G + kc + 1]).then_inc(hT_hi, 1)
            act.activation(lam_z, par[:, LAMBDA:LAMBDA + LC], ACT.Abs).then_inc(lam_exp, 1)
            his(1)
            act.wait_ge(lam_exp, 1)
            act.activation(lam_u, lam_z, ACT.Exp, scale=-1.0).then_inc(lam_exp, 1)
            his(2, 3)
            for c in range(LC):
                act.wait_ge(unit_used, U_X + c + 1)
                w3 = CONV_W + (LRU_CONV - 1) * LC + c
                act.activation(xc[:, c, :], bank[c][:, 0:SEQ], ACT.Identity, bias=par[:, CONV_B + c:CONV_B + c + 1],
                               scale=par[:, w3:w3 + 1]).then_inc(conv_base, 1)
                his(U_Q + c)
            his(8)
            def squares(m, u, b):
                act.wait_ge(unit_used, u)
                if m >= 1:
                    act.wait_ge(qk_sum, m)
                act.activation(sq_tok, bank[b][:, :], ACT.Square).then_inc(qk_sq, 1)

            squares(0, U_K, 4)
            his(9)
            squares(1, U_K, 5)
            for c in range(LC):
                act.wait_ge(gates_done, c + 1)
                act.activation(gate_r[:, c, :], bank[c][:, 0:SEQ], ACT.Sigmoid,
                               bias=par[:, B_A + c:B_A + c + 1])
                act.activation(gate_i[:, c, :], bank[c][:, SEQ:2 * SEQ], ACT.Sigmoid,
                               bias=par[:, B_I + c:B_I + c + 1]).then_inc(gates_read, 1)
                if c == 1:
                    his(10)
            his(11)
            act.wait_ge(log_c_done, 1)
            act.wait_ge(gates_read, LC)
            for c in range(LC):
                act.activation(decay[:, c, :], gate_r[:, c, :], ACT.Exp, scale=log_c[:, c:c + 1])
                act.activation(tanh_a[:, c, :], gate_r[:, c, :], ACT.Tanh,
                               scale=log_c[:, c:c + 1]).then_inc(decay_done, 1)
            his(12)
            act.wait_ge(decay_done, LC)
            act.activation(flat(gate_r), flat(decay), ACT.Square).then_inc(a2_done, 1)
            squares(2, U_Y, 6)
            his(13)
            squares(3, U_Y, 7)
            act.wait_ge(qk_sum, 4)
            act.activation(qk_rms, qk_ss, ACT.Sqrt, bias=eps, scale=1.0 / HEAD_DIM).then_inc(qk_rms_done, 1)
            act.wait_ge(one_m_a2, 1)
            act.activation(flat(tanh_a), flat(tanh_a), ACT.Sqrt, scale=-1.0).then_inc(root_done, 1)
            his(14, 15)
            act.wait_ge(q_scale_done, 1)
            for c in range(LC):
                act.wait_ge(qkT, c + 1)
                act.activation(q_T[:, c, :], bank[QK_T[c]][:, 0:SEQ], ACT.Copy, scale=q_scale[:, c:c + 1])
                act.activation(k_T[:, c, :], bank[QK_T[c]][:, SEQ:2 * SEQ], ACT.Copy,
                               scale=par[:, K_G:K_G + 1]).then_inc(qkT_read, 1)
                if c == 1:
                    his(16)
            his(17)
            for j in range(2):
                act.wait_ge(unit_used, U_Y + 2 * j + 2)
                act.activation(ygate[:, 2 * j:2 * j + 2, :], bank[j][:, :].rearrange("p (c t) -> p c t", c=2),
                               ACT.Gelu_apprx_tanh).then_inc(ygate_done, 1)

            def exps(h):
                act.wait_ge(shifted, h + 1)
                for m in range(TT):
                    part = slice(KEY_AT[m], KEY_AT[m] + KEYS[m])
                    act.activation(probs[h % 4][:, part], probs[h % 4][:, part], ACT.Exp, scale=-1.0,
                                   bias=neg_max[:, h, m:m + 1],
                                   accum_out=row_sum[:, h, m:m + 1]).then_inc(probs_done, 1)

            def p_out(h):
                act.wait_ge(pT, h + 1)
                act.activation(p_T[:, h, :], bank[2 + h % 2][:, 0:SCORES], ACT.Copy).then_inc(pT_read, 1)

            exps(0)
            exps(1)
            his(18)
            act.wait_ge(y_done, 1)
            act.activation(flat(xc), flat(ygate), ACT.Square).then_inc(y_sq, 1)
            his(19)
            p_out(0)
            p_out(1)
            exps(2)
            exps(3)
            his(20)
            p_out(2)
            p_out(3)
            exps(4)
            exps(5)
            his(21)
            p_out(4)
            p_out(5)
            his(22)
            exps(6)
            exps(7)
            act.wait_ge(y_sum, 1)
            act.activation(y_rms, bank[2][:, 0:TT], ACT.Sqrt, bias=eps, scale=1.0 / LRU_WIDTH).then_inc(y_rms_done, 1)
            his(23)
            p_out(6)
            p_out(7)
            for m in range(TT):
                act.wait_ge(unit_used, U_O)
                act.activation(v_tok[:, m, :], bank[6 + m][:, :], ACT.Copy).then_inc(v_ready, 1)
            his(24)
            for m in range(TT):
                act.wait_ge(attn_out, m + 1)
                act.activation(sq_tok, y_attn[m], ACT.Square, accum_out=a_ss[:, m:m + 1]).then_inc(a_sq, 1)
                act.wait_ge(a_sq, m + 1)
                act.activation(a_rms[:, m:m + 1], a_ss[:, m:m + 1], ACT.Sqrt, bias=eps,
                               scale=1.0 / ATTN_WIDTH).then_inc(a_rms_done, 1)
            his(25)
            for c in range(LC):
                act.wait_ge(aT, c // 2 + 1)
                act.activation(mix_hi[:, LC + c, :], bank[2 + c // 2][:, SEQ * (c % 2):SEQ * (c % 2 + 1)], ACT.Copy,
                               scale=par[:, ATTN_G + c:ATTN_G + c + 1]).then_inc(aT_hi, 1)
            his(26, 27)
            for m in range(TT):
                hi(U_FFN + m, ffn_unit(0, "gv"[m]))
                for n in range(2):
                    act.wait_ge(x2_done, 2 * m + n + 1)
                    if m or n:
                        act.wait_ge(f_sq, 2 * m + n)
                    act.activation(sq_tok, x_tok[:, m, 512 * n:512 * (n + 1)], ACT.Square,
                                   accum_out=f_ss[:, 2 * m + n:2 * m + n + 1]).then_inc(f_sq, 1)
                act.wait_ge(f_added, m + 1)
                act.activation(f_rms[:, m:m + 1], f_sum[:, m:m + 1], ACT.Sqrt, bias=eps,
                               scale=1.0 / D_MODEL).then_inc(f_rms_done, 1)
            for j in range(KC // 2):
                act.wait_ge(fT, j + 1)
                for kc in (2 * j, 2 * j + 1):
                    act.activation(h_hi[:, kc, :], f_at(kc), ACT.Copy,
                                   scale=par[:, FFN_G + kc:FFN_G + kc + 1]).then_inc(fT_hi, 1)

            def ffn_base(s, which, it=None):
                u = ffn_units(s)[which][0]
                act.wait_ge(unit_used, at_pass(it, LOOP_UNITS, u + 1))
                col = at_pass(it, LOOP_STEPS, s + which * STEPS)
                act.activation((conv_g, conv_v)[which][s % 2], up_bank(s, which)[:, 0:SEQ], ACT.Identity,
                               bias=fpar_b[:, bass.ds(col + 2 * STEPS, 1)],
                               scale=fpar_b[:, bass.ds(col, 1)]).then_inc(up_base, 1)

            def ffn_gelu(s, it=None):
                act.wait_ge(conv_g_done, at_pass(it, LOOP_STEPS, s + 1))
                act.activation(gelu_g[s % 2], conv_g[s % 2], ACT.Gelu_apprx_tanh).then_inc(gelu_done, 1)

            def ffn_step(t, it=None):
                g, v, down = [(u, ffn_unit(s, kind)) for u, s, kind in ffn_units(t)]
                hi(*g, it)
                ffn_base(t - 1, 0, it)
                hi(*v, it)
                ffn_base(t - 1, 1, it)
                hi(*down, it)
                ffn_gelu(t - 1, it)

            ffn_step(1)
            with act.Fori(0, LOOPS) as it:
                for t in range(2, 2 + LOOP_STEPS):
                    ffn_step(t, it)
            hi(U_LAST, ffn_unit(STEPS - 1, "d"))
            ffn_base(STEPS - 1, 0)
            ffn_base(STEPS - 1, 1)
            ffn_gelu(STEPS - 1)

        @block.vector
        def _(dve):
            links = [0]

            def link(ins):
                links[0] += 1
                ins.then_inc(chain, 1)
                dve.wait_ge(chain, links[0])

            def lo(u, raw_unit, it=None):
                _, src, by_cols = raw_unit
                dve.wait_ge(hi_done, at_pass(it, LOOP_UNITS, u + 1))
                dve.tensor_tensor(as_unit(w_lo[u % RING], by_cols), src,
                                  as_unit(w_hi[u % RING], by_cols).bitcast(F32),
                                  ALU.subtract).then_inc(lo_done, 1)

            def los(*units):
                for u in units:
                    lo(u, head_unit(u))

            def make_diag(rms, rstd, m, done):
                link(dve.reciprocal(rstd[:, m:m + 1], rms[:, m:m + 1]))
                dve.tensor_scalar(diag[:, m, :], ident[:, :], rstd[:, m:m + 1], None, ALU.mult).then_inc(done, 1)

            dve.wait_ge(x_landed[1], 16)
            dve.tensor_tensor_reduce(flat(tanh_a), x_tok[:, 1, :], x_tok[:, 1, :], 1.0, 0.0, ALU.mult, ALU.add,
                                     x_ss[:, 1:2]).then_inc(x_sq_1, 1)
            dve.wait_ge(par_T, 1)
            dve.tensor_copy(par[:, :], bank[7][:, 0:N_PAR]).then_inc(par_ready, 1)
            dve.tensor_copy(fpar_a[:, :], bank[7][:, 64:64 + N_FPAR]).then_inc(par_ready, 1)
            dve.tensor_copy(fpar_b[:, :], bank[7][:, 192:192 + N_FPAR]).then_inc(par_ready, 1)
            dve.wait_ge(consts, 2)
            for m in range(TT):
                dve.wait_ge(x_rms_done, m + 1)
                make_diag(x_rms, x_rstd, m, diag_done)
            los(0)
            for kc in range(KC):
                dve.wait_ge(hT_hi, kc + 1)
                dve.scalar_tensor_tensor(h_lo[:, kc, :], bank[kc][:, 0:SEQ], par[:, MIX_G + kc:MIX_G + kc + 1],
                                         h_hi[:, kc, :].bitcast(F32), ALU.mult, ALU.subtract).then_inc(hT_lo, 1)
            los(1)
            dve.wait_ge(dist_done, TT + HEADS)
            dve.tensor_scalar(q_scale, q_scale, par[:, Q_G:Q_G + 1], None, ALU.mult).then_inc(q_scale_done, 1)
            los(2)
            dve.wait_ge(lam_exp, 2)
            link(dve.tensor_scalar(lam_z, lam_u, 2.0, None, ALU.add))
            link(dve.reciprocal(lam_z2, lam_z))
            link(dve.tensor_tensor(lam_z, lam_u, lam_z2, ALU.mult))
            link(dve.tensor_tensor(lam_z2, lam_z, lam_z, ALU.mult))
            link(dve.tensor_scalar(lam_s, lam_z2, 1.0 / 17, None, ALU.mult))
            for k in range(7, 0, -1):
                link(dve.scalar_tensor_tensor(lam_s, lam_s, 1.0 / (2 * k + 1), lam_z2, ALU.add, ALU.mult))
            link(dve.scalar_tensor_tensor(lam_s, lam_s, 1.0, lam_z, ALU.add, ALU.mult))
            link(dve.tensor_scalar(lam_p, par[:, LAMBDA:LAMBDA + LC], -1.0, 0.0, ALU.mult, ALU.max))
            link(dve.scalar_tensor_tensor(lam_p, lam_s, 2.0, lam_p, ALU.mult, ALU.add))
            dve.tensor_scalar(log_c, lam_p, -LRU_C, None, ALU.mult).then_inc(log_c_done, 1)
            los(3)
            for c in range(LC):
                dve.wait_ge(conv_base, c + 1)
                for back in range(1, LRU_CONV):
                    col = CONV_W + (LRU_CONV - 1 - back) * LC + c
                    tap = dve.scalar_tensor_tensor(xc[:, c, back:SEQ], bank[c][:, 0:SEQ - back], par[:, col:col + 1],
                                                   xc[:, c, back:SEQ], ALU.mult, ALU.add)
                    if back < LRU_CONV - 1:
                        link(tap)
                tap.then_inc(conv_done, 1)
                los(U_Q + c)

            def head_sums(g):
                dve.wait_ge(qk_sq, g + 1)
                dve.tensor_reduce(qk_ss[:, g, :], sq_tok.rearrange("p (h d) -> p h d", h=HEADS), AX_X,
                                  ALU.add).then_inc(qk_sum, 1)

            los(8)
            head_sums(0)
            los(9)
            head_sums(1)
            los(10)
            dve.wait_ge(gates_read, LC)
            dve.wait_ge(conv_done, LC)
            dve.tensor_tensor(flat(gate_i), flat(gate_i), flat(xc), ALU.mult).then_inc(lru_in, 1)
            los(11, 12)
            dve.wait_ge(a2_done, 1)
            dve.scalar_tensor_tensor(flat(tanh_a), flat(gate_r), 1.0, flat(tanh_a), ALU.add,
                                     ALU.mult).then_inc(one_m_a2, 1)
            head_sums(2)
            los(13)
            head_sums(3)
            dve.wait_ge(qk_rms_done, 1)
            link(dve.reciprocal(qk_rstd, qk_rms))
            for g in range(2 * TT):
                dve.tensor_tensor(qk_tok[:, g, :].rearrange("p (h d) -> p h d", h=HEADS),
                                  bank[4 + g][:, :].rearrange("p (h d) -> p h d", h=HEADS),
                                  qk_rstd[:, g, :].unsqueeze(2).to_broadcast([P, HEADS, HEAD_DIM]),
                                  ALU.mult).then_inc(qk_norm, 1)
            los(14)
            dve.wait_ge(root_done, 1)
            dve.wait_ge(lru_in, 1)
            link(dve.tensor_tensor(flat(gate_r), flat(tanh_a), flat(gate_i), ALU.mult))
            los(15)
            for c in range(LC):
                dve.tensor_tensor_scan(tanh_a[:, c, :], decay[:, c, :], gate_r[:, c, :], 0.0, ALU.mult,
                                       ALU.add).then_inc(scan_done, 1)
            los(16, 17)
            dve.wait_ge(ygate_done, 2)
            dve.wait_ge(scan_done, LC)
            dve.tensor_tensor(flat(ygate), flat(tanh_a), flat(ygate), ALU.mult).then_inc(y_done, 1)

            def shift(h):
                dve.wait_ge(scores, h + 1)
                if h == 0:
                    dve.wait_ge(dist_done, TT)
                if h >= 4:
                    dve.wait_ge(pT, h - 3)
                for m in range(TT):
                    part = slice(KEY_AT[m], KEY_AT[m] + KEYS[m])
                    ins = dve.tensor_tensor_reduce(probs[h % 4][:, part], bank[4 + h % 2][:, part], neg_dist[:, part],
                                                   -slope(h), 3.4e38, ALU.add, ALU.min, neg_max[:, h, m:m + 1])
                ins.then_inc(shifted, 1)

            shift(0)
            shift(1)
            los(18)
            shift(2)
            shift(3)
            los(19)
            shift(4)
            shift(5)
            los(20)
            shift(6)
            shift(7)
            los(21)
            dve.wait_ge(y_rms_done, 1)
            for m in range(TT):
                make_diag(y_rms, y_rstd, m, y_diag)
            los(22)
            dve.wait_ge(y_bc, 1)
            for c in range(LC):
                dve.scalar_tensor_tensor(decay[:, c, :], ygate[:, c, :], par[:, LRU_G + c:LRU_G + c + 1],
                                         bank[2][:, SEQ:2 * SEQ], ALU.mult, ALU.mult).then_inc(y_scaled, 1)
            dve.wait_ge(y_scaled, LC)
            link(dve.tensor_copy(mix_hi[:, 0:LC, :], decay[:, :, :]))
            dve.tensor_tensor(mix_lo[:, 0:LC, :], decay[:, :, :], mix_hi[:, 0:LC, :].bitcast(F32),
                              ALU.subtract).then_inc(mix_ready, 1)
            los(23)
            dve.wait_ge(probs_done, HEADS * TT)
            link(dve.reciprocal(row_rec, row_sum))
            los(24)
            dve.wait_ge(o_done, 1)
            for m in range(TT):
                dve.tensor_tensor(y_attn[m].rearrange("p (h d) -> p h d", h=HEADS),
                                  bank[6 + m][:, :].rearrange("p (h d) -> p h d", h=HEADS),
                                  row_rec[:, :, m:m + 1].to_broadcast([P, HEADS, HEAD_DIM]),
                                  ALU.mult).then_inc(attn_out, 1)
            for m in range(TT):
                dve.wait_ge(a_rms_done, m + 1)
                make_diag(a_rms, a_rstd, m, a_diag)
            los(25)
            for j in range(2):
                dve.wait_ge(aT_hi, 2 * j + 2)
                for c in (2 * j, 2 * j + 1):
                    dve.scalar_tensor_tensor(mix_lo[:, LC + c, :], bank[2 + j][:, SEQ * (c % 2):SEQ * (c % 2 + 1)],
                                             par[:, ATTN_G + c:ATTN_G + c + 1],
                                             mix_hi[:, LC + c, :].bitcast(F32),
                                             ALU.mult, ALU.subtract).then_inc(mix_ready, 1)
            los(26, 27)
            for m in range(TT):
                lo(U_FFN + m, ffn_unit(0, "gv"[m]))
                for n in range(2):
                    half = slice(512 * n, 512 * (n + 1))
                    if m == TT - 1 and n == 1:
                        dve.wait_ge(unit_used, U_FFN)
                    else:
                        dve.wait_ge(wout_done, 2 * m + n + 1)
                    dve.tensor_tensor(x_tok[:, m, half], x_tok[:, m, half], bank[O_ACC[2 * m + n]][:, :],
                                      ALU.add).then_inc(x2_done, 1)
                dve.wait_ge(f_sq, 2 * m + 2)
                dve.tensor_tensor(f_sum[:, m:m + 1], f_ss[:, 2 * m:2 * m + 1], f_ss[:, 2 * m + 1:2 * m + 2],
                                  ALU.add).then_inc(f_added, 1)
                dve.wait_ge(f_rms_done, m + 1)
                make_diag(f_rms, f_rstd, m, f_diag)
            for kc in range(KC):
                if kc % 2 == 0:
                    dve.wait_ge(fT_hi, kc + 2)
                dve.scalar_tensor_tensor(h_lo[:, kc, :], f_at(kc), par[:, FFN_G + kc:FFN_G + kc + 1],
                                         h_hi[:, kc, :].bitcast(F32), ALU.mult, ALU.subtract).then_inc(fT_lo, 1)

            def ffn_taps(s, which, tapped, done, it=None):
                dve.wait_ge(up_base, at_pass(it, 2 * LOOP_STEPS, 2 * s + which + 1))
                acc, col = (conv_g, conv_v)[which][s % 2], at_pass(it, LOOP_STEPS, s + which * STEPS)
                dve.scalar_tensor_tensor(acc[:, 1:SEQ], up_bank(s, which)[:, 0:SEQ - 1],
                                         fpar_a[:, bass.ds(col + 2 * STEPS, 1)], acc[:, 1:SEQ],
                                         ALU.mult, ALU.add).then_inc(tapped, 1)
                dve.wait_ge(tapped, at_pass(it, LOOP_STEPS, s + 1))
                dve.scalar_tensor_tensor(acc[:, 2:SEQ], up_bank(s, which)[:, 0:SEQ - 2],
                                         fpar_a[:, bass.ds(col, 1)], acc[:, 2:SEQ],
                                         ALU.mult, ALU.add).then_inc(done, 1)

            def ffn_act(s, it=None):
                count = at_pass(it, LOOP_STEPS, s + 1)
                dve.wait_ge(gelu_done, count)
                dve.wait_ge(conv_v_done, count)
                dve.tensor_tensor(prod[s % 2], gelu_g[s % 2], conv_v[s % 2], ALU.mult).then_inc(prod_done, 1)
                if s >= 1:
                    dve.wait_ge(unit_used, at_pass(it, LOOP_UNITS, U_FFN - 1 + 3 * s))
                dve.wait_ge(prod_done, count)
                dve.tensor_copy(act_hi[:, s % 2, :], prod[s % 2]).then_inc(act_hi_done, 1)
                dve.wait_ge(act_hi_done, count)
                dve.tensor_tensor(act_lo[:, s % 2, :], prod[s % 2], act_hi[:, s % 2, :].bitcast(F32),
                                  ALU.subtract).then_inc(act_ready, 1)

            def ffn_step(t, it=None):
                g, v, down = [(u, ffn_unit(s, kind)) for u, s, kind in ffn_units(t)]
                lo(*g, it)
                ffn_taps(t - 1, 0, tap_g, conv_g_done, it)
                lo(*v, it)
                ffn_taps(t - 1, 1, tap_v, conv_v_done, it)
                lo(*down, it)
                ffn_act(t - 1, it)

            ffn_step(1)
            with dve.Fori(0, LOOPS) as it:
                for t in range(2, 2 + LOOP_STEPS):
                    ffn_step(t, it)
            lo(U_LAST, ffn_unit(STEPS - 1, "d"))
            ffn_taps(STEPS - 1, 0, tap_g, conv_g_done)
            ffn_taps(STEPS - 1, 1, tap_v, conv_v_done)
            ffn_act(STEPS - 1)
            for m in range(TT):
                for n in range(2):
                    half = slice(512 * n, 512 * (n + 1))
                    dve.wait_ge(down_done, 2 * m + n + 1)
                    dve.tensor_tensor(x_tok[:, m, half], x_tok[:, m, half], bank[DOWN[2 * m + n]][:, :],
                                      ALU.add).then_inc(final, 1)

        @block.tensor
        def _(pe):
            def three(acc, lhs_hi, lhs_lo, rhs_hi, rhs_lo, first, last):
                pe.matmul(acc, lhs_hi, rhs_hi, start=first, stop=False)
                pe.matmul(acc, lhs_hi, rhs_lo, start=False, stop=False)
                return pe.matmul(acc, lhs_lo, rhs_hi, start=False, stop=last)

            def split(u, it=None):
                pe.wait_ge(lo_done, at_pass(it, LOOP_UNITS, u + 1))

            def cols_unit(u, acc, h_ready=None, it=None):
                split(u, it)
                whi, wlo = as_unit(w_hi[u % RING], True), as_unit(w_lo[u % RING], True)
                for kc in range(KC):
                    if h_ready is not None:
                        pe.wait_ge(h_ready, kc + 1)
                    ins = three(acc, whi[:, kc, :], wlo[:, kc, :], h_hi[:, kc, :], h_lo[:, kc, :],
                                kc == 0, kc == KC - 1)
                ins.then_inc(unit_used, 1)

            def rows_unit(u, first_unit, banks):
                split(u)
                for k in range(2):
                    kc, cols = 2 * (u - first_unit) + k, slice(512 * k, 512 * (k + 1))
                    for m in range(TT):
                        tok = slice(P * m, P * (m + 1))
                        ins = three(banks[m][:, :], h_hi[:, kc, tok], h_lo[:, kc, tok],
                                    w_hi[u % RING][:, cols], w_lo[u % RING][:, cols], kc == 0, kc == KC - 1)
                ins.then_inc(unit_used, 1)

            def down_like(u, banks, m, lhs_hi, lhs_lo, first, last):
                tok = slice(P * m, P * (m + 1))
                return [three(banks[2 * m + n][:, :], lhs_hi[:, tok], lhs_lo[:, tok],
                              w_hi[u % RING][:, 512 * n:512 * (n + 1)], w_lo[u % RING][:, 512 * n:512 * (n + 1)],
                              first, last) for n in range(2)]

            pe.wait_ge(consts, 2)
            pe.wait_ge(par_landed, 16 * 13)
            pe.transpose(bank[7][:, 0:N_PAR], rows[0][0:N_PAR], ident[0:N_PAR, 0:N_PAR])
            pe.wait_ge(fpar_landed, 16 * 3)
            for k in range(2):
                ins = pe.transpose(bank[7][:, 64 + 128 * k:64 + 128 * k + N_FPAR], rows[1 + k][0:N_FPAR],
                                   ident[0:N_FPAR, 0:N_FPAR])
            ins.then_inc(par_T, 1)
            pe.wait_ge(diag_done, TT)
            for kc in range(KC):
                if kc == 7:
                    pe.wait_ge(par_ready, 3)
                for m in range(TT):
                    ins = pe.matmul(bank[kc][:, P * m:P * (m + 1)], x_tok[:, m, P * kc:P * (kc + 1)],
                                    diag[:, m, :], start=True, stop=True)
                ins.then_inc(xT, 1)
            for c in range(LC):
                cols_unit(U_X + c, bank[c][:, 0:SEQ], hT_lo)
            for j in range(4):
                rows_unit(U_Q + j, U_Q, bank[4:6])
            pe.wait_ge(gates_landed, 16 * 4)
            for c in range(LC):
                pe.wait_ge(conv_done, c + 1)
                pe.matmul(bank[c][:, 0:SEQ], w_gate[:, 0, c, :], xc[:, c, :], start=True, stop=True)
                pe.matmul(bank[c][:, SEQ:2 * SEQ], w_gate[:, 1, c, :], xc[:, c, :], start=True,
                          stop=True).then_inc(gates_done, 1)
            for j in range(4):
                rows_unit(U_K + j, U_K, bank[6:8])
            pe.wait_ge(gates_read, LC)
            for c in range(LC):
                cols_unit(U_Y + c, bank[c // 2][:, SEQ * (c % 2):SEQ * (c % 2 + 1)])
            def transpose_qk(c):
                if c == 0:
                    pe.wait_ge(qk_norm, 2 * TT)
                for g in range(2 * TT):
                    ins = pe.transpose(bank[QK_T[c]][:, P * g:P * (g + 1)], qk_tok[:, g, P * c:P * (c + 1)],
                                       ident[:, :])
                ins.then_inc(qkT, 1)

            def score(h):
                c, rows_h = h // 2, slice(HEAD_DIM * (h % 2), HEAD_DIM * (h % 2 + 1))
                if h == 0:
                    pe.wait_ge(qkT_read, LC)
                if h >= 2:
                    pe.wait_ge(shifted, h - 1)
                for m in range(TT):
                    ins = pe.matmul(bank[4 + h % 2][:, KEY_AT[m]:KEY_AT[m] + KEYS[m]],
                                    q_T[rows_h, c, P * m:P * (m + 1)], k_T[rows_h, c, 0:KEYS[m]],
                                    start=True, stop=True)
                ins.then_inc(scores, 1)

            def transpose_p(h):
                pe.wait_ge(probs_done, TT * (h + 1))
                if h >= 2:
                    pe.wait_ge(pT_read, h - 1)
                if h == 6:
                    pe.wait_ge(y_scaled, LC)
                for b in range(SCORES // P):
                    ins = pe.transpose(bank[2 + h % 2][:, P * b:P * (b + 1)], probs[h % 4][:, P * b:P * (b + 1)],
                                       ident[:, :])
                ins.then_inc(pT, 1)

            for c in range(LC):
                transpose_qk(c)
            for h in range(2):
                score(h)
            for j in range(4):
                rows_unit(U_V + j, U_V, bank[6:8])
                if j < 3:
                    score(2 * j + 2)
                    score(2 * j + 3)
                    transpose_p(2 * j)
                    transpose_p(2 * j + 1)
            pe.wait_ge(y_sq, 1)
            pe.wait_ge(pT_read, 5)
            for m in range(TT):
                for c in range(LC):
                    ins = pe.matmul(bank[2][:, m:m + 1], xc[:, c, P * m:P * (m + 1)], ones[:, 0:1],
                                    start=(c == 0), stop=(c == LC - 1))
            ins.then_inc(y_sum, 1)
            pe.wait_ge(y_diag, TT)
            for m in range(TT):
                ins = pe.matmul(bank[2][:, SEQ + P * m:SEQ + P * (m + 1)], ones[:, :], diag[:, m, :],
                                start=True, stop=True)
            ins.then_inc(y_bc, 1)
            transpose_p(6)
            transpose_p(7)

            def out_unit(u, m):
                kc = u - U_O
                return down_like(u, [bank[b] for b in O_ACC], m, mix_hi[:, kc, :], mix_lo[:, kc, :],
                                 kc == 0, kc == KC - 1)

            pe.wait_ge(ygate_done, 2)
            pe.wait_ge(shifted, HEADS)
            pe.wait_ge(mix_ready, 1)
            for j in range(LC):
                u = U_O + j
                split(u)
                for m in range(TT):
                    ins = out_unit(u, m)[-1]
                ins.then_inc(unit_used, 1)
                if j == 0:
                    pe.wait_ge(v_ready, TT)
                    pe.wait_ge(pT_read, HEADS)
                    for h in range(HEADS):
                        dst = slice(HEAD_DIM * h, HEAD_DIM * (h + 1))
                        pe.matmul(bank[6][:, dst], p_T[:, h, 0:P], v_tok[:, 0, dst], start=True, stop=True)
                        pe.matmul(bank[7][:, dst], p_T[:, h, P:2 * P], v_tok[:, 0, dst], start=True, stop=False)
                        ins = pe.matmul(bank[7][:, dst], p_T[:, h, 2 * P:3 * P], v_tok[:, 1, dst],
                                        start=False, stop=True)
                    ins.then_inc(o_done, 1)
            pe.wait_ge(a_diag, TT)
            for c in range(LC):
                for m in range(TT):
                    at = SEQ * (c % 2) + P * m
                    ins = pe.matmul(bank[2 + c // 2][:, at:at + P], y_attn[m][:, P * c:P * (c + 1)],
                                    diag[:, m, :], start=True, stop=True)
                if c % 2 == 1:
                    ins.then_inc(aT, 1)

            def transpose_f(m):
                pe.wait_ge(f_diag, m + 1)
                for kc in range(KC):
                    ins = pe.matmul(f_at(kc)[:, P * m:P * (m + 1)], x_tok[:, m, P * kc:P * (kc + 1)], diag[:, m, :],
                                    start=True, stop=True)
                    if m == TT - 1 and kc % 2 == 1:
                        ins.then_inc(fT, 1)

            for m in range(TT):
                for j in range(LC, KC):
                    u = U_O + j
                    split(u)
                    if m == 0:
                        pe.wait_ge(mix_ready, 1 + j - LC + 1)
                    first, second = out_unit(u, m)
                    if j == KC - 1:
                        first.then_inc(wout_done, 1)
                    if m == 0 and j == KC - 1:
                        second.then_inc(wout_done, 1)
                    elif m == 1:
                        second.then_inc(unit_used, 1)
                    if m == 1 and j == KC - 2:
                        transpose_f(0)
            transpose_f(1)

            def ffn_up(s, it=None):
                for which, (u, _, _) in enumerate(ffn_units(s)[0:2]):
                    if s >= 2:
                        pe.wait_ge((conv_g_done, conv_v_done)[which], at_pass(it, LOOP_STEPS, s - 1))
                    cols_unit(u, up_bank(s, which)[:, 0:SEQ], fT_lo if s == 0 and which == 0 else None, it)

            def ffn_down(s, u, it=None):
                split(u, it)
                pe.wait_ge(act_ready, at_pass(it, LOOP_STEPS, s + 1))
                for m in range(TT):
                    ends = down_like(u, [bank[b] for b in DOWN], m, act_hi[:, s % 2, :], act_lo[:, s % 2, :],
                                     s == 0, s == STEPS - 1)
                    if s == STEPS - 1:
                        for end in ends:
                            end.then_inc(down_done, 1)
                if s < STEPS - 1:
                    ends[-1].then_inc(unit_used, 1)

            ffn_up(0)
            for t in range(1, 2):
                ffn_up(t)
                ffn_down(t - 1, ffn_units(t)[2][0])
            with pe.Fori(0, LOOPS) as it:
                for t in range(2, 2 + LOOP_STEPS):
                    ffn_up(t, it)
                    ffn_down(t - 1, ffn_units(t)[2][0], it)
            ffn_down(STEPS - 1, U_LAST)


_INS = ['x', 'mix_norm_g', 'w_in', 'lru_conv_w', 'lru_conv_b', 'lru_w_a', 'lru_b_a', 'lru_w_i', 'lru_b_i',
        'lru_lambda', 'q_norm_g', 'k_norm_g', 'lru_out_g', 'attn_out_g', 'w_out', 'ffn_norm_g', 'w_up',
        'ffn_conv_w', 'ffn_conv_b', 'w_down']


def kernel(**inputs):
    import numpy as _np
    import concourse.bacc as _bacc
    from concourse import mybir as _mybir
    from concourse.bass_utils import run_bass_kernel_spmd as _run

    nc = _bacc.Bacc("TRN2", target_bir_lowering=False, num_devices=1)
    arrays, args = {}, []
    for name in _INS:
        a = _np.ascontiguousarray(inputs[name])
        arrays[f"in_{name}_dram"] = a
        args.append(nc.dram_tensor(f"in_{name}_dram", a.shape, _mybir.dt.from_np(a.dtype), kind="ExternalInput").ap())
    args.append(nc.dram_tensor("out_0_dram", (1, SEQ, D_MODEL), _mybir.dt.float32, kind="ExternalOutput").ap())
    build_layer(nc, *args)
    r = _run(nc, [arrays], core_ids=[0])
    return r.results[0]["out_0_dram"]
```

```python
from contextlib import ExitStack

import concourse.bass as bass
from concourse import mybir

F32 = mybir.dt.float32
F32R = mybir.dt.float32r
ACT = mybir.ActivationFunctionType
ALU = mybir.AluOpType
AX_X = mybir.AxisListType.X

P = 128
D_MODEL = 1024
SEQ = 256
LRU_WIDTH = 512
LRU_HEADS = 8
LRU_HEAD_DIM = LRU_WIDTH // LRU_HEADS
LRU_CONV = 4
LRU_C = 8.0
ATTN_WIDTH = 512
HEADS = 8
HEAD_DIM = ATTN_WIDTH // HEADS
D_FF = 2816
FFN_CONV = 3
EPS = 1e-6

KC = D_MODEL // P
TT = SEQ // P
LC = LRU_WIDTH // P
STEPS = D_FF // P
UNIT = 1024
RAW = 6
RING = 6
MASKED = -3.0e38
KEYS = [P, 2 * P]
KEY_AT = [0, P]
SCORES = sum(KEYS)

U_X, U_Q, U_K, U_Y, U_V, U_O = 0, 4, 8, 12, 16, 20
U_FFN = 28
LOOP_STEPS = 4
LOOPS = (STEPS - 2) // LOOP_STEPS
LOOP_UNITS = 3 * LOOP_STEPS
U_LOOP = U_FFN + 5
U_LAST = U_LOOP + LOOPS * LOOP_UNITS
UNITS = U_LAST + 1
DMAS = UNITS // 2
assert (STEPS - 2) % LOOP_STEPS == 0 and LOOP_UNITS % RING == 0 and LOOP_UNITS == 2 * RAW and UNITS % 2 == 0

MIX_G, CONV_W, CONV_B, B_A, B_I, LAMBDA = 0, 8, 24, 28, 32, 36
LRU_G, ATTN_G, FFN_G, Q_G, K_G = 40, 44, 48, 56, 57
FFN_W, FFN_B = 58, 58 + FFN_CONV * 2 * STEPS
N_PAR = FFN_B + 2 * STEPS


def build_layer(nc, x, stream, params, gates, out):
    with ExitStack() as ctx:
        def sb(name, shape, dt=F32):
            return ctx.enter_context(nc.sbuf_tensor(name, shape, dt))

        def sem(name):
            return ctx.enter_context(nc.semaphore(name))

        bank = [ctx.enter_context(nc.psum_tensor(f"bank{b}", [P, 512], F32)) for b in range(8)]
        raw = [sb(f"raw{r}", [P, 2 * UNIT]) for r in range(RAW)]
        w_hi = [sb(f"w_hi{r}", [P, UNIT], F32R) for r in range(RING)]
        w_lo = [sb(f"w_lo{r}", [P, UNIT], F32R) for r in range(RING)]
        x_tok = sb("x_tok", [P, TT, D_MODEL])
        h_hi = sb("h_hi", [P, KC, SEQ], F32R)
        h_lo = sb("h_lo", [P, KC, SEQ], F32R)
        mix_hi = sb("mix_hi", [P, KC, SEQ], F32R)
        mix_lo = sb("mix_lo", [P, KC, SEQ], F32R)
        xc = sb("xc", [P, LC, SEQ])
        gate_r = sb("gate_r", [P, LC, SEQ])
        gate_i = sb("gate_i", [P, LC, SEQ])
        decay = sb("decay", [P, LC, SEQ])
        tanh_a = sb("tanh_a", [P, LC, SEQ])
        ygate = sb("ygate", [P, LC, SEQ])
        qk_tok = sb("qk_tok", [P, 2 * TT, ATTN_WIDTH])
        q_T = sb("q_T", [P, LC, SEQ])
        k_T = sb("k_T", [P, LC, SEQ])
        v_tok = sb("v_tok", [P, TT, ATTN_WIDTH])
        p_T = sb("p_T", [P, HEADS, SCORES])
        act_hi = sb("act_hi", [P, 2, SEQ], F32R)
        act_lo = sb("act_lo", [P, 2, SEQ], F32R)
        neg_dist = sb("neg_dist", [P, SCORES])
        ident = sb("ident", [P, P])
        ones = sb("ones", [P, P])
        diag = sb("diag", [P, TT, P])
        par = sb("par", [P, N_PAR])
        small = sb("small", [P, 200])
        probs = [qk_tok[:, :, :].rearrange("p a b -> p (a b)")[:, SCORES * j:SCORES * (j + 1)]
                 for j in range(4)]
        conv_g = [xc[:, j, :] for j in range(2)]
        conv_v = [xc[:, 2 + j, :] for j in range(2)]
        gelu_g = [gate_r[:, j, :] for j in range(2)]
        prod = [gate_i[:, j, :] for j in range(2)]
        y_attn = [q_T[:, :, :].rearrange("p c t -> p (c t)")[:, 0:512],
                  q_T[:, :, :].rearrange("p c t -> p (c t)")[:, 512:1024]]
        w_gate = p_T[:, 4:8, :].rearrange("p h s -> p (h s)")[:, 0:2 * LC * P].rearrange(
            "p (g c j) -> p g c j", g=2, c=LC)

        def flat(t):
            return t[:, :, :].rearrange("p c t -> p (c t)")

        x_norm = [flat(decay), flat(gate_i)]
        sq_tok = flat(p_T)[:, 2560:3072]
        eps = small[:, 0:1]
        x_ss, x_rms, x_rstd = small[:, 2:4], small[:, 4:6], small[:, 6:8]
        lam_u, lam_z, lam_z2, lam_s, log_c = (small[:, 8 + 4 * j:12 + 4 * j] for j in range(5))
        row_sum = small[:, 28:44].rearrange("p (h m) -> p h m", m=TT)
        neg_max = small[:, 44:60].rearrange("p (h m) -> p h m", m=TT)
        row_rec = small[:, 60:76].rearrange("p (h m) -> p h m", m=TT)
        q_scale = small[:, 76:80]
        y_rms, y_rstd = small[:, 80:82], small[:, 82:84]
        a_ss, a_rms, a_rstd = small[:, 84:86], small[:, 86:88], small[:, 88:90]
        f_ss, f_sum, f_rms, f_rstd = small[:, 90:94], small[:, 94:96], small[:, 96:98], small[:, 98:100]
        lam_p = small[:, 100:104]
        warm_out = small[:, 1:2]
        qk_ss, qk_rms, qk_rstd = (small[:, 104 + 32 * j:136 + 32 * j].rearrange("p (g h) -> p g h", h=HEADS)
                                  for j in range(3))

        raw_landed = [sem(f"raw_landed{r}") for r in range(RAW)]
        x_landed = [sem(f"x_landed{m}") for m in range(TT)]
        par_landed, first_landed = sem("par_landed"), sem("first_landed")
        gates_landed = sem("gates_landed")
        out_stored = sem("out_stored")
        hi_done, lo_done, unit_used = sem("hi_done"), sem("lo_done"), sem("unit_used")
        consts = sem("consts")
        dist_done = sem("dist_done")
        warm, x_normed = sem("warm"), sem("x_normed")
        x_sq, x_sq_1 = sem("x_sq"), sem("x_sq_1")
        q_scale_done, f_added = sem("q_scale_done"), sem("f_added")
        x_rms_done, x_rec = sem("x_rms_done"), sem("x_rec")
        xT, hT_hi, hT_lo = sem("xT"), sem("hT_hi"), sem("hT_lo")
        conv_base, conv_done = sem("conv_base"), sem("conv_done")
        gates_done, gates_read = sem("gates_done"), sem("gates_read")
        lam_exp, log_c_done = sem("lam_exp"), sem("log_c_done")
        decay_done, a2_done, one_m_a2, root_done = sem("decay_done"), sem("a2_done"), sem("one_m_a2"), sem("root_done")
        lru_in, scan_done = sem("lru_in"), sem("scan_done")
        ygate_done, y_done, y_sq = sem("ygate_done"), sem("y_done"), sem("y_sq")
        y_sum, y_rms_done, y_diag, y_bc = sem("y_sum"), sem("y_rms_done"), sem("y_diag"), sem("y_bc")
        y_scaled, mix_ready = sem("y_scaled"), sem("mix_ready")
        qk_sq, qk_sum, qk_rms_done, qk_norm = sem("qk_sq"), sem("qk_sum"), sem("qk_rms_done"), sem("qk_norm")
        qkT, qkT_read = sem("qkT"), sem("qkT_read")
        v_ready = sem("v_ready")
        scores, shifted, probs_done = sem("scores"), sem("shifted"), sem("probs_done")
        pT, pT_read = sem("pT"), sem("pT_read")
        o_done, attn_out, a_sq, a_rms_done, a_normed = (
            sem("o_done"), sem("attn_out"), sem("a_sq"), sem("a_rms_done"), sem("a_normed"))
        aT, aT_hi = sem("aT"), sem("aT_hi")
        wout_done, x2_done, f_sq, f_rms_done, f_rec, f_normed = (
            sem("wout_done"), sem("x2_done"), sem("f_sq"), sem("f_rms_done"), sem("f_rec"), sem("f_normed"))
        fT, fT_hi, fT_lo = sem("fT"), sem("fT_hi"), sem("fT_lo")
        up_base, conv_g_done, conv_v_done, gelu_done, act_ready = (
            sem("up_base"), sem("conv_g_done"), sem("conv_v_done"), sem("gelu_done"), sem("act_ready"))
        tap_g, tap_v, prod_done, act_hi_done = sem("tap_g"), sem("tap_v"), sem("prod_done"), sem("act_hi_done")
        chain = sem("chain")
        pool_chain = sem("pool_chain")
        down_done, final = sem("down_done"), sem("final")

        def raw_unit(u):
            return raw[(u // 2) % RAW][:, UNIT * (u % 2):UNIT * (u % 2 + 1)]

        def by_chunk(tile):
            return tile[:, :].rearrange("p (kc n) -> p kc n", kc=KC)

        def ffn_units(s):
            if s == 0:
                return [U_FFN, U_FFN + 1]
            return [U_FFN + 3 * s - 1 + k for k in range(3)]

        def up_bank(s, which):
            return bank[(0, 1, 4, 5)[2 * (s % 2) + which]]

        DOWN = (2, 3, 6, 7)
        O_ACC = (0, 1, 4, 5)
        QK_T = (2, 3, 4, 5)

        def f_at(kc):
            return bank[DOWN[kc // 2]][:, SEQ * (kc % 2):SEQ * (kc % 2 + 1)]

        def slope(h):
            return 2.0 ** (-8.0 * (h + 1) / HEADS)

        def at_pass(it, per, value):
            return value if it is None else it * per + value

        block = ctx.enter_context(nc.Block())

        @block.sync
        def _(sp):
            x_t = x[0].rearrange("(m p) d -> m p d", p=P)
            for m in range(TT):
                sp.dma_start(x_tok[:, m, :], x_t[m]).then_inc(x_landed[m], 16)

            sp.dma_start(raw[0][:, 0:UNIT], stream[0, :, 0:UNIT]).then_inc(first_landed, 16)
            sp.dma_start(raw[0][:, UNIT:2 * UNIT], stream[0, :, UNIT:2 * UNIT]).then_inc(raw_landed[0], 16)
            for n in range(1, RAW):
                sp.dma_start(raw[n][:, :], stream[n]).then_inc(raw_landed[n], 16)

            def reload(n, units_split):
                sp.wait_ge(lo_done, units_split)
                if isinstance(n, int):
                    src = stream[n]
                else:
                    src = stream[bass.ds(n, 1)].rearrange("one p c -> (one p) c")
                return src

            with sp.Fori(0, DMAS // RAW - 1) as it:
                for r in range(RAW):
                    src = reload(it * RAW + (RAW + r), it * (2 * RAW) + (2 * r + 2))
                    sp.dma_start(raw[r][:, :], src).then_inc(raw_landed[r], 16)
            for n in range(DMAS - DMAS % RAW, DMAS):
                src = reload(n, 2 * (n - RAW) + 2)
                sp.dma_start(raw[n % RAW][:, :], src).then_inc(raw_landed[n % RAW], 16)
            out_t = out[0].rearrange("(m p) d -> m p d", p=P)
            for m in range(TT):
                for n in range(2):
                    sp.wait_ge(final, 2 * m + n + 1)
                    sp.dma_start(out_t[m][:, 512 * n:512 * (n + 1)],
                                 x_tok[:, m, 512 * n:512 * (n + 1)]).then_inc(out_stored, 16)
            sp.wait_ge(out_stored, 16 * 2 * TT)

        @block.gpsimd
        def _(pool):
            pool.dma_start(par[:, :], params).then_inc(par_landed, 16)
            pool.dma_start(w_gate.rearrange("p g c j -> p (g c j)"), gates).then_inc(gates_landed, 16)
            pool.memset(ones[:, :], 1.0).then_inc(pool_chain, 1)
            pool.memset(eps, EPS).then_inc(consts, 1)
            pool.wait_ge(pool_chain, 1)
            pool.affine_select(out=ident[:, :], in_=ones[:, :], compare_op=ALU.is_equal, fill=0.0, base=0,
                               pattern=[[-1, P]], channel_multiplier=1).then_inc(consts, 1)
            for m in range(TT):
                view = neg_dist[:, KEY_AT[m]:KEY_AT[m] + KEYS[m]]
                pool.iota(view, pattern=[[1, KEYS[m]]], base=-P * m, channel_multiplier=-1,
                          allow_small_or_imprecise_dtypes=True).then_inc(pool_chain, 1)
                pool.wait_ge(pool_chain, 2 + m)
                pool.affine_select(out=view, in_=view, compare_op=ALU.is_ge, fill=MASKED, base=P * m,
                                   pattern=[[-1, KEYS[m]]], channel_multiplier=1).then_inc(dist_done, 1)
            for h in range(HEADS):
                half = HEAD_DIM * (h % 2)
                pool.wait_ge(dist_done, TT + h)
                pool.memset(q_scale[half:half + HEAD_DIM, h // 2:h // 2 + 1],
                            HEAD_DIM ** -0.5 / slope(h)).then_inc(dist_done, 1)

        @block.scalar
        def _(act):
            def hi(u, it=None):
                if u == 0:
                    act.wait_ge(first_landed, 16)
                else:
                    act.wait_ge(raw_landed[(u // 2) % RAW], at_pass(it, 16, 16 * (u // 2 // RAW + 1)))
                if u >= RING:
                    act.wait_ge(unit_used, at_pass(it, LOOP_UNITS, u - RING + 1))
                act.activation(w_hi[u % RING][:, :], raw_unit(u), ACT.Copy).then_inc(hi_done, 1)

            def his(*units):
                for u in units:
                    hi(u)

            act.wait_ge(consts, 1)
            act.activation(warm_out, eps, ACT.Sqrt).then_inc(warm, 1)
            act.wait_ge(x_landed[0], 16)
            act.activation(flat(ygate), x_tok[:, 0, :], ACT.Square, accum_out=x_ss[:, 0:1]).then_inc(x_sq, 1)
            for m in range(TT):
                if m == 0:
                    act.wait_ge(x_sq, 1)
                else:
                    act.wait_ge(x_sq_1, 1)
                act.activation(x_rms[:, m:m + 1], x_ss[:, m:m + 1], ACT.Sqrt, bias=eps,
                               scale=1.0 / D_MODEL).then_inc(x_rms_done, 1)
            act.wait_ge(x_rec, 1)
            act.activation(x_norm[0], x_tok[:, 0, :], ACT.Copy, scale=x_rstd[:, 0:1]).then_inc(x_normed, 1)
            his(0)
            act.wait_ge(par_landed, 16)
            for kc in range(KC):
                act.wait_ge(xT, kc + 1)
                act.activation(h_hi[:, kc, :], bank[kc][:, 0:SEQ], ACT.Copy,
                               scale=par[:, MIX_G + kc:MIX_G + kc + 1]).then_inc(hT_hi, 1)
            act.activation(lam_z, par[:, LAMBDA:LAMBDA + LC], ACT.Abs).then_inc(lam_exp, 1)
            his(1)
            act.wait_ge(lam_exp, 1)
            act.activation(lam_u, lam_z, ACT.Exp, scale=-1.0).then_inc(lam_exp, 1)
            his(2, 3)
            for c in range(LC):
                act.wait_ge(unit_used, U_X + c + 1)
                w3 = CONV_W + (LRU_CONV - 1) * LC + c
                act.activation(xc[:, c, :], bank[c][:, 0:SEQ], ACT.Identity, bias=par[:, CONV_B + c:CONV_B + c + 1],
                               scale=par[:, w3:w3 + 1]).then_inc(conv_base, 1)
                his(U_Q + c)
            his(8)
            def squares(m, u, b):
                act.wait_ge(unit_used, u)
                if m >= 1:
                    act.wait_ge(qk_sum, m)
                act.activation(sq_tok, bank[b][:, :], ACT.Square).then_inc(qk_sq, 1)

            squares(0, U_K, 4)
            his(9)
            squares(1, U_K, 5)
            for c in range(LC):
                act.wait_ge(gates_done, c + 1)
                act.activation(gate_r[:, c, :], bank[c][:, 0:SEQ], ACT.Sigmoid,
                               bias=par[:, B_A + c:B_A + c + 1])
                act.activation(gate_i[:, c, :], bank[c][:, SEQ:2 * SEQ], ACT.Sigmoid,
                               bias=par[:, B_I + c:B_I + c + 1]).then_inc(gates_read, 1)
                if c == 1:
                    his(10)
            his(11)
            act.wait_ge(log_c_done, 1)
            act.wait_ge(gates_read, LC)
            for c in range(LC):
                act.activation(decay[:, c, :], gate_r[:, c, :], ACT.Exp, scale=log_c[:, c:c + 1])
                act.activation(tanh_a[:, c, :], gate_r[:, c, :], ACT.Tanh,
                               scale=log_c[:, c:c + 1]).then_inc(decay_done, 1)
            his(12)
            act.wait_ge(decay_done, LC)
            act.activation(flat(gate_r), flat(decay), ACT.Square).then_inc(a2_done, 1)
            squares(2, U_Y, 6)
            his(13)
            squares(3, U_Y, 7)
            act.wait_ge(qk_sum, 4)
            act.activation(qk_rms, qk_ss, ACT.Sqrt, bias=eps, scale=1.0 / HEAD_DIM).then_inc(qk_rms_done, 1)
            act.wait_ge(one_m_a2, 1)
            act.activation(flat(tanh_a), flat(tanh_a), ACT.Sqrt, scale=-1.0).then_inc(root_done, 1)
            his(14, 15)
            act.wait_ge(q_scale_done, 1)
            for c in range(LC):
                act.wait_ge(qkT, c + 1)
                act.activation(q_T[:, c, :], bank[QK_T[c]][:, 0:SEQ], ACT.Copy, scale=q_scale[:, c:c + 1])
                act.activation(k_T[:, c, :], bank[QK_T[c]][:, SEQ:2 * SEQ], ACT.Copy,
                               scale=par[:, K_G:K_G + 1]).then_inc(qkT_read, 1)
                if c == 1:
                    his(16)
            his(17)
            for j in range(2):
                act.wait_ge(unit_used, U_Y + 2 * j + 2)
                act.activation(ygate[:, 2 * j:2 * j + 2, :], bank[j][:, :].rearrange("p (c t) -> p c t", c=2),
                               ACT.Gelu_apprx_tanh).then_inc(ygate_done, 1)

            def exps(h):
                act.wait_ge(shifted, h + 1)
                for m in range(TT):
                    part = slice(KEY_AT[m], KEY_AT[m] + KEYS[m])
                    act.activation(probs[h % 4][:, part], probs[h % 4][:, part], ACT.Exp, scale=-1.0,
                                   bias=neg_max[:, h, m:m + 1],
                                   accum_out=row_sum[:, h, m:m + 1]).then_inc(probs_done, 1)

            def p_out(h):
                act.wait_ge(pT, h + 1)
                act.activation(p_T[:, h, :], bank[2 + h % 2][:, 0:SCORES], ACT.Copy).then_inc(pT_read, 1)

            exps(0)
            exps(1)
            his(18)
            act.wait_ge(y_done, 1)
            act.activation(flat(xc), flat(ygate), ACT.Square).then_inc(y_sq, 1)
            his(19)
            p_out(0)
            p_out(1)
            exps(2)
            exps(3)
            his(20)
            p_out(2)
            p_out(3)
            exps(4)
            exps(5)
            his(21)
            p_out(4)
            p_out(5)
            his(22)
            exps(6)
            exps(7)
            act.wait_ge(y_sum, 1)
            act.activation(y_rms, bank[2][:, 0:TT], ACT.Sqrt, bias=eps, scale=1.0 / LRU_WIDTH).then_inc(y_rms_done, 1)
            his(23)
            p_out(6)
            p_out(7)
            for m in range(TT):
                act.wait_ge(unit_used, U_O)
                act.activation(v_tok[:, m, :], bank[6 + m][:, :], ACT.Copy).then_inc(v_ready, 1)
            his(24)
            for m in range(TT):
                act.wait_ge(attn_out, m + 1)
                act.activation(sq_tok, y_attn[m], ACT.Square, accum_out=a_ss[:, m:m + 1]).then_inc(a_sq, 1)
                act.wait_ge(a_sq, m + 1)
                act.activation(a_rms[:, m:m + 1], a_ss[:, m:m + 1], ACT.Sqrt, bias=eps,
                               scale=1.0 / ATTN_WIDTH).then_inc(a_rms_done, 1)
            his(25)
            for c in range(LC):
                act.wait_ge(aT, c // 2 + 1)
                act.activation(mix_hi[:, LC + c, :], bank[2 + c // 2][:, SEQ * (c % 2):SEQ * (c % 2 + 1)], ACT.Copy,
                               scale=par[:, ATTN_G + c:ATTN_G + c + 1]).then_inc(aT_hi, 1)
            his(26, 27)
            for m in range(TT):
                hi(U_FFN + m)
                for n in range(2):
                    act.wait_ge(x2_done, 2 * m + n + 1)
                    if m or n:
                        act.wait_ge(f_sq, 2 * m + n)
                    act.activation(sq_tok, x_tok[:, m, 512 * n:512 * (n + 1)], ACT.Square,
                                   accum_out=f_ss[:, 2 * m + n:2 * m + n + 1]).then_inc(f_sq, 1)
                act.wait_ge(f_added, m + 1)
                act.activation(f_rms[:, m:m + 1], f_sum[:, m:m + 1], ACT.Sqrt, bias=eps,
                               scale=1.0 / D_MODEL).then_inc(f_rms_done, 1)
                act.wait_ge(f_rec, m + 1)
                act.activation(x_norm[m][:, 0:512], x_tok[:, m, 0:512], ACT.Copy,
                               scale=f_rstd[:, m:m + 1]).then_inc(f_normed, 1)
            for j in range(KC // 2):
                act.wait_ge(fT, j + 1)
                for kc in (2 * j, 2 * j + 1):
                    act.activation(h_hi[:, kc, :], f_at(kc), ACT.Copy,
                                   scale=par[:, FFN_G + kc:FFN_G + kc + 1]).then_inc(fT_hi, 1)

            def ffn_base(s, which, it=None):
                u = ffn_units(s)[which]
                act.wait_ge(unit_used, at_pass(it, LOOP_UNITS, u + 1))
                col = at_pass(it, LOOP_STEPS, s + which * STEPS)
                act.activation((conv_g, conv_v)[which][s % 2], up_bank(s, which)[:, 0:SEQ], ACT.Identity,
                               bias=par[:, bass.ds(col + FFN_B, 1)],
                               scale=par[:, bass.ds(col + (FFN_W + 4 * STEPS), 1)]).then_inc(up_base, 1)

            def ffn_gelu(s, it=None):
                act.wait_ge(conv_g_done, at_pass(it, LOOP_STEPS, s + 1))
                act.activation(gelu_g[s % 2], conv_g[s % 2], ACT.Gelu_apprx_tanh).then_inc(gelu_done, 1)

            def ffn_step(t, it=None):
                g, v, down = ffn_units(t)
                hi(g, it)
                ffn_base(t - 1, 0, it)
                hi(v, it)
                ffn_base(t - 1, 1, it)
                hi(down, it)
                ffn_gelu(t - 1, it)

            ffn_step(1)
            with act.Fori(0, LOOPS) as it:
                for t in range(2, 2 + LOOP_STEPS):
                    ffn_step(t, it)
            hi(U_LAST)
            ffn_base(STEPS - 1, 0)
            ffn_base(STEPS - 1, 1)
            ffn_gelu(STEPS - 1)

        @block.vector
        def _(dve):
            links = [0]

            def link(ins):
                links[0] += 1
                ins.then_inc(chain, 1)
                dve.wait_ge(chain, links[0])

            def lo(u, it=None):
                dve.wait_ge(hi_done, at_pass(it, LOOP_UNITS, u + 1))
                dve.tensor_tensor(w_lo[u % RING][:, :], raw_unit(u), w_hi[u % RING][:, :].bitcast(F32),
                                  ALU.subtract).then_inc(lo_done, 1)

            def los(*units):
                for u in units:
                    lo(u)

            def make_diag(rms, rstd, m, done):
                link(dve.reciprocal(rstd[:, m:m + 1], rms[:, m:m + 1]))
                dve.tensor_scalar(diag[:, m, :], ident[:, :], rstd[:, m:m + 1], None, ALU.mult).then_inc(done, 1)

            dve.wait_ge(x_landed[1], 16)
            dve.tensor_tensor_reduce(flat(tanh_a), x_tok[:, 1, :], x_tok[:, 1, :], 1.0, 0.0, ALU.mult, ALU.add,
                                     x_ss[:, 1:2]).then_inc(x_sq_1, 1)
            for m in range(TT):
                dve.wait_ge(x_rms_done, m + 1)
                dve.reciprocal(x_rstd[:, m:m + 1], x_rms[:, m:m + 1]).then_inc(x_rec, 1)
            dve.wait_ge(x_rec, TT)
            dve.tensor_scalar(x_norm[1], x_tok[:, 1, :], x_rstd[:, 1:2], None, ALU.mult).then_inc(x_normed, 1)
            los(0)
            for kc in range(KC):
                dve.wait_ge(hT_hi, kc + 1)
                dve.scalar_tensor_tensor(h_lo[:, kc, :], bank[kc][:, 0:SEQ], par[:, MIX_G + kc:MIX_G + kc + 1],
                                         h_hi[:, kc, :].bitcast(F32), ALU.mult, ALU.subtract).then_inc(hT_lo, 1)
            los(1)
            dve.wait_ge(dist_done, TT + HEADS)
            dve.tensor_scalar(q_scale, q_scale, par[:, Q_G:Q_G + 1], None, ALU.mult).then_inc(q_scale_done, 1)
            los(2)
            dve.wait_ge(lam_exp, 2)
            link(dve.tensor_scalar(lam_z, lam_u, 2.0, None, ALU.add))
            link(dve.reciprocal(lam_z2, lam_z))
            link(dve.tensor_tensor(lam_z, lam_u, lam_z2, ALU.mult))
            link(dve.tensor_tensor(lam_z2, lam_z, lam_z, ALU.mult))
            link(dve.tensor_scalar(lam_s, lam_z2, 1.0 / 17, None, ALU.mult))
            for k in range(7, 0, -1):
                link(dve.scalar_tensor_tensor(lam_s, lam_s, 1.0 / (2 * k + 1), lam_z2, ALU.add, ALU.mult))
            link(dve.scalar_tensor_tensor(lam_s, lam_s, 1.0, lam_z, ALU.add, ALU.mult))
            link(dve.tensor_scalar(lam_p, par[:, LAMBDA:LAMBDA + LC], -1.0, 0.0, ALU.mult, ALU.max))
            link(dve.scalar_tensor_tensor(lam_p, lam_s, 2.0, lam_p, ALU.mult, ALU.add))
            dve.tensor_scalar(log_c, lam_p, -LRU_C, None, ALU.mult).then_inc(log_c_done, 1)
            los(3)
            for c in range(LC):
                dve.wait_ge(conv_base, c + 1)
                for back in range(1, LRU_CONV):
                    col = CONV_W + (LRU_CONV - 1 - back) * LC + c
                    tap = dve.scalar_tensor_tensor(xc[:, c, back:SEQ], bank[c][:, 0:SEQ - back], par[:, col:col + 1],
                                                   xc[:, c, back:SEQ], ALU.mult, ALU.add)
                    if back < LRU_CONV - 1:
                        link(tap)
                tap.then_inc(conv_done, 1)
                los(U_Q + c)

            def head_sums(g):
                dve.wait_ge(qk_sq, g + 1)
                dve.tensor_reduce(qk_ss[:, g, :], sq_tok.rearrange("p (h d) -> p h d", h=HEADS), AX_X,
                                  ALU.add).then_inc(qk_sum, 1)

            los(8)
            head_sums(0)
            los(9)
            head_sums(1)
            los(10)
            dve.wait_ge(gates_read, LC)
            dve.wait_ge(conv_done, LC)
            dve.tensor_tensor(flat(gate_i), flat(gate_i), flat(xc), ALU.mult).then_inc(lru_in, 1)
            los(11, 12)
            dve.wait_ge(a2_done, 1)
            dve.scalar_tensor_tensor(flat(tanh_a), flat(gate_r), 1.0, flat(tanh_a), ALU.add,
                                     ALU.mult).then_inc(one_m_a2, 1)
            head_sums(2)
            los(13)
            head_sums(3)
            dve.wait_ge(qk_rms_done, 1)
            link(dve.reciprocal(qk_rstd, qk_rms))
            for g in range(2 * TT):
                dve.tensor_tensor(qk_tok[:, g, :].rearrange("p (h d) -> p h d", h=HEADS),
                                  bank[4 + g][:, :].rearrange("p (h d) -> p h d", h=HEADS),
                                  qk_rstd[:, g, :].unsqueeze(2).to_broadcast([P, HEADS, HEAD_DIM]),
                                  ALU.mult).then_inc(qk_norm, 1)
            los(14)
            dve.wait_ge(root_done, 1)
            dve.wait_ge(lru_in, 1)
            link(dve.tensor_tensor(flat(gate_r), flat(tanh_a), flat(gate_i), ALU.mult))
            los(15)
            for c in range(LC):
                dve.tensor_tensor_scan(tanh_a[:, c, :], decay[:, c, :], gate_r[:, c, :], 0.0, ALU.mult,
                                       ALU.add).then_inc(scan_done, 1)
            los(16, 17)
            dve.wait_ge(ygate_done, 2)
            dve.wait_ge(scan_done, LC)
            dve.tensor_tensor(flat(ygate), flat(tanh_a), flat(ygate), ALU.mult).then_inc(y_done, 1)

            def shift(h):
                dve.wait_ge(scores, h + 1)
                if h == 0:
                    dve.wait_ge(dist_done, TT)
                if h >= 4:
                    dve.wait_ge(pT, h - 3)
                for m in range(TT):
                    part = slice(KEY_AT[m], KEY_AT[m] + KEYS[m])
                    ins = dve.tensor_tensor_reduce(probs[h % 4][:, part], bank[4 + h % 2][:, part], neg_dist[:, part],
                                                   -slope(h), 3.4e38, ALU.add, ALU.min, neg_max[:, h, m:m + 1])
                ins.then_inc(shifted, 1)

            shift(0)
            shift(1)
            los(18)
            shift(2)
            shift(3)
            los(19)
            shift(4)
            shift(5)
            los(20)
            shift(6)
            shift(7)
            los(21)
            dve.wait_ge(consts, 2)
            dve.wait_ge(y_rms_done, 1)
            for m in range(TT):
                make_diag(y_rms, y_rstd, m, y_diag)
            los(22)
            dve.wait_ge(y_bc, 1)
            for c in range(LC):
                dve.scalar_tensor_tensor(decay[:, c, :], ygate[:, c, :], par[:, LRU_G + c:LRU_G + c + 1],
                                         bank[2][:, SEQ:2 * SEQ], ALU.mult, ALU.mult).then_inc(y_scaled, 1)
            dve.wait_ge(y_scaled, LC)
            link(dve.tensor_copy(mix_hi[:, 0:LC, :], decay[:, :, :]))
            dve.tensor_tensor(mix_lo[:, 0:LC, :], decay[:, :, :], mix_hi[:, 0:LC, :].bitcast(F32),
                              ALU.subtract).then_inc(mix_ready, 1)
            los(23)
            dve.wait_ge(probs_done, HEADS * TT)
            link(dve.reciprocal(row_rec, row_sum))
            los(24)
            dve.wait_ge(o_done, 1)
            for m in range(TT):
                dve.tensor_tensor(y_attn[m].rearrange("p (h d) -> p h d", h=HEADS),
                                  bank[6 + m][:, :].rearrange("p (h d) -> p h d", h=HEADS),
                                  row_rec[:, :, m:m + 1].to_broadcast([P, HEADS, HEAD_DIM]),
                                  ALU.mult).then_inc(attn_out, 1)
            for m in range(TT):
                dve.wait_ge(a_rms_done, m + 1)
                link(dve.reciprocal(a_rstd[:, m:m + 1], a_rms[:, m:m + 1]))
                dve.tensor_scalar(y_attn[m], y_attn[m], a_rstd[:, m:m + 1], None, ALU.mult).then_inc(a_normed, 1)
            los(25)
            for j in range(2):
                dve.wait_ge(aT_hi, 2 * j + 2)
                for c in (2 * j, 2 * j + 1):
                    dve.scalar_tensor_tensor(mix_lo[:, LC + c, :], bank[2 + j][:, SEQ * (c % 2):SEQ * (c % 2 + 1)],
                                             par[:, ATTN_G + c:ATTN_G + c + 1],
                                             mix_hi[:, LC + c, :].bitcast(F32),
                                             ALU.mult, ALU.subtract).then_inc(mix_ready, 1)
            los(26, 27)
            for m in range(TT):
                lo(U_FFN + m)
                for n in range(2):
                    half = slice(512 * n, 512 * (n + 1))
                    if m == TT - 1 and n == 1:
                        dve.wait_ge(unit_used, U_FFN)
                    else:
                        dve.wait_ge(wout_done, 2 * m + n + 1)
                    dve.tensor_tensor(x_tok[:, m, half], x_tok[:, m, half], bank[O_ACC[2 * m + n]][:, :],
                                      ALU.add).then_inc(x2_done, 1)
                dve.wait_ge(f_sq, 2 * m + 2)
                dve.tensor_tensor(f_sum[:, m:m + 1], f_ss[:, 2 * m:2 * m + 1], f_ss[:, 2 * m + 1:2 * m + 2],
                                  ALU.add).then_inc(f_added, 1)
                dve.wait_ge(f_rms_done, m + 1)
                dve.reciprocal(f_rstd[:, m:m + 1], f_rms[:, m:m + 1]).then_inc(f_rec, 1)
                dve.wait_ge(f_rec, m + 1)
                dve.tensor_scalar(x_norm[m][:, 512:1024], x_tok[:, m, 512:1024], f_rstd[:, m:m + 1], None,
                                  ALU.mult).then_inc(f_normed, 1)
            for kc in range(KC):
                if kc % 2 == 0:
                    dve.wait_ge(fT_hi, kc + 2)
                dve.scalar_tensor_tensor(h_lo[:, kc, :], f_at(kc), par[:, FFN_G + kc:FFN_G + kc + 1],
                                         h_hi[:, kc, :].bitcast(F32), ALU.mult, ALU.subtract).then_inc(fT_lo, 1)

            def ffn_taps(s, which, tapped, done, it=None):
                dve.wait_ge(up_base, at_pass(it, 2 * LOOP_STEPS, 2 * s + which + 1))
                acc, col = (conv_g, conv_v)[which][s % 2], at_pass(it, LOOP_STEPS, s + which * STEPS)
                dve.scalar_tensor_tensor(acc[:, 1:SEQ], up_bank(s, which)[:, 0:SEQ - 1],
                                         par[:, bass.ds(col + (FFN_W + 2 * STEPS), 1)], acc[:, 1:SEQ],
                                         ALU.mult, ALU.add).then_inc(tapped, 1)
                dve.wait_ge(tapped, at_pass(it, LOOP_STEPS, s + 1))
                dve.scalar_tensor_tensor(acc[:, 2:SEQ], up_bank(s, which)[:, 0:SEQ - 2],
                                         par[:, bass.ds(col + FFN_W, 1)], acc[:, 2:SEQ],
                                         ALU.mult, ALU.add).then_inc(done, 1)

            def ffn_act(s, it=None):
                count = at_pass(it, LOOP_STEPS, s + 1)
                dve.wait_ge(gelu_done, count)
                dve.wait_ge(conv_v_done, count)
                dve.tensor_tensor(prod[s % 2], gelu_g[s % 2], conv_v[s % 2], ALU.mult).then_inc(prod_done, 1)
                if s >= 1:
                    dve.wait_ge(unit_used, at_pass(it, LOOP_UNITS, U_FFN - 1 + 3 * s))
                dve.wait_ge(prod_done, count)
                dve.tensor_copy(act_hi[:, s % 2, :], prod[s % 2]).then_inc(act_hi_done, 1)
                dve.wait_ge(act_hi_done, count)
                dve.tensor_tensor(act_lo[:, s % 2, :], prod[s % 2], act_hi[:, s % 2, :].bitcast(F32),
                                  ALU.subtract).then_inc(act_ready, 1)

            def ffn_step(t, it=None):
                g, v, down = ffn_units(t)
                lo(g, it)
                ffn_taps(t - 1, 0, tap_g, conv_g_done, it)
                lo(v, it)
                ffn_taps(t - 1, 1, tap_v, conv_v_done, it)
                lo(down, it)
                ffn_act(t - 1, it)

            ffn_step(1)
            with dve.Fori(0, LOOPS) as it:
                for t in range(2, 2 + LOOP_STEPS):
                    ffn_step(t, it)
            lo(U_LAST)
            ffn_taps(STEPS - 1, 0, tap_g, conv_g_done)
            ffn_taps(STEPS - 1, 1, tap_v, conv_v_done)
            ffn_act(STEPS - 1)
            for m in range(TT):
                for n in range(2):
                    half = slice(512 * n, 512 * (n + 1))
                    dve.wait_ge(down_done, 2 * m + n + 1)
                    dve.tensor_tensor(x_tok[:, m, half], x_tok[:, m, half], bank[DOWN[2 * m + n]][:, :],
                                      ALU.add).then_inc(final, 1)

        @block.tensor
        def _(pe):
            def three(acc, lhs_hi, lhs_lo, rhs_hi, rhs_lo, first, last):
                pe.matmul(acc, lhs_hi, rhs_hi, start=first, stop=False)
                pe.matmul(acc, lhs_hi, rhs_lo, start=False, stop=False)
                return pe.matmul(acc, lhs_lo, rhs_hi, start=False, stop=last)

            def split(u, it=None):
                pe.wait_ge(lo_done, at_pass(it, LOOP_UNITS, u + 1))

            def cols_unit(u, acc, h_ready=None, it=None):
                split(u, it)
                whi, wlo = by_chunk(w_hi[u % RING]), by_chunk(w_lo[u % RING])
                for kc in range(KC):
                    if h_ready is not None:
                        pe.wait_ge(h_ready, kc + 1)
                    ins = three(acc, whi[:, kc, :], wlo[:, kc, :], h_hi[:, kc, :], h_lo[:, kc, :],
                                kc == 0, kc == KC - 1)
                ins.then_inc(unit_used, 1)

            def rows_unit(u, first_unit, banks):
                split(u)
                for k in range(2):
                    kc, cols = 2 * (u - first_unit) + k, slice(512 * k, 512 * (k + 1))
                    for m in range(TT):
                        tok = slice(P * m, P * (m + 1))
                        ins = three(banks[m][:, :], h_hi[:, kc, tok], h_lo[:, kc, tok],
                                    w_hi[u % RING][:, cols], w_lo[u % RING][:, cols], kc == 0, kc == KC - 1)
                ins.then_inc(unit_used, 1)

            def down_like(u, banks, m, lhs_hi, lhs_lo, first, last):
                tok = slice(P * m, P * (m + 1))
                return [three(banks[2 * m + n][:, :], lhs_hi[:, tok], lhs_lo[:, tok],
                              w_hi[u % RING][:, 512 * n:512 * (n + 1)], w_lo[u % RING][:, 512 * n:512 * (n + 1)],
                              first, last) for n in range(2)]

            pe.wait_ge(consts, 2)
            pe.wait_ge(x_normed, TT)
            for kc in range(KC):
                for m in range(TT):
                    ins = pe.transpose(bank[kc][:, P * m:P * (m + 1)], x_norm[m][:, P * kc:P * (kc + 1)], ident[:, :])
                ins.then_inc(xT, 1)
            for c in range(LC):
                cols_unit(U_X + c, bank[c][:, 0:SEQ], hT_lo)
            for j in range(4):
                rows_unit(U_Q + j, U_Q, bank[4:6])
            pe.wait_ge(gates_landed, 16)
            for c in range(LC):
                pe.wait_ge(conv_done, c + 1)
                pe.matmul(bank[c][:, 0:SEQ], w_gate[:, 0, c, :], xc[:, c, :], start=True, stop=True)
                pe.matmul(bank[c][:, SEQ:2 * SEQ], w_gate[:, 1, c, :], xc[:, c, :], start=True,
                          stop=True).then_inc(gates_done, 1)
            for j in range(4):
                rows_unit(U_K + j, U_K, bank[6:8])
            pe.wait_ge(gates_read, LC)
            for c in range(LC):
                cols_unit(U_Y + c, bank[c // 2][:, SEQ * (c % 2):SEQ * (c % 2 + 1)])
            def transpose_qk(c):
                if c == 0:
                    pe.wait_ge(qk_norm, 2 * TT)
                for g in range(2 * TT):
                    ins = pe.transpose(bank[QK_T[c]][:, P * g:P * (g + 1)], qk_tok[:, g, P * c:P * (c + 1)],
                                       ident[:, :])
                ins.then_inc(qkT, 1)

            def score(h):
                c, rows_h = h // 2, slice(HEAD_DIM * (h % 2), HEAD_DIM * (h % 2 + 1))
                if h == 0:
                    pe.wait_ge(qkT_read, LC)
                if h >= 2:
                    pe.wait_ge(shifted, h - 1)
                for m in range(TT):
                    ins = pe.matmul(bank[4 + h % 2][:, KEY_AT[m]:KEY_AT[m] + KEYS[m]],
                                    q_T[rows_h, c, P * m:P * (m + 1)], k_T[rows_h, c, 0:KEYS[m]],
                                    start=True, stop=True)
                ins.then_inc(scores, 1)

            def transpose_p(h):
                pe.wait_ge(probs_done, TT * (h + 1))
                if h >= 2:
                    pe.wait_ge(pT_read, h - 1)
                if h == 6:
                    pe.wait_ge(y_scaled, LC)
                for b in range(SCORES // P):
                    ins = pe.transpose(bank[2 + h % 2][:, P * b:P * (b + 1)], probs[h % 4][:, P * b:P * (b + 1)],
                                       ident[:, :])
                ins.then_inc(pT, 1)

            for c in range(LC):
                transpose_qk(c)
            for h in range(2):
                score(h)
            for j in range(4):
                rows_unit(U_V + j, U_V, bank[6:8])
                if j < 3:
                    score(2 * j + 2)
                    score(2 * j + 3)
                    transpose_p(2 * j)
                    transpose_p(2 * j + 1)
            pe.wait_ge(y_sq, 1)
            pe.wait_ge(pT_read, 5)
            for m in range(TT):
                for c in range(LC):
                    ins = pe.matmul(bank[2][:, m:m + 1], xc[:, c, P * m:P * (m + 1)], ones[:, 0:1],
                                    start=(c == 0), stop=(c == LC - 1))
            ins.then_inc(y_sum, 1)
            pe.wait_ge(y_diag, TT)
            for m in range(TT):
                ins = pe.matmul(bank[2][:, SEQ + P * m:SEQ + P * (m + 1)], ones[:, :], diag[:, m, :],
                                start=True, stop=True)
            ins.then_inc(y_bc, 1)
            transpose_p(6)
            transpose_p(7)

            def out_unit(u, m):
                kc = u - U_O
                return down_like(u, [bank[b] for b in O_ACC], m, mix_hi[:, kc, :], mix_lo[:, kc, :],
                                 kc == 0, kc == KC - 1)

            pe.wait_ge(ygate_done, 2)
            pe.wait_ge(shifted, HEADS)
            pe.wait_ge(mix_ready, 1)
            for j in range(LC):
                u = U_O + j
                split(u)
                for m in range(TT):
                    ins = out_unit(u, m)[-1]
                ins.then_inc(unit_used, 1)
                if j == 0:
                    pe.wait_ge(v_ready, TT)
                    pe.wait_ge(pT_read, HEADS)
                    for h in range(HEADS):
                        dst = slice(HEAD_DIM * h, HEAD_DIM * (h + 1))
                        pe.matmul(bank[6][:, dst], p_T[:, h, 0:P], v_tok[:, 0, dst], start=True, stop=True)
                        pe.matmul(bank[7][:, dst], p_T[:, h, P:2 * P], v_tok[:, 0, dst], start=True, stop=False)
                        ins = pe.matmul(bank[7][:, dst], p_T[:, h, 2 * P:3 * P], v_tok[:, 1, dst],
                                        start=False, stop=True)
                    ins.then_inc(o_done, 1)
            pe.wait_ge(a_normed, TT)
            for c in range(LC):
                for m in range(TT):
                    at = SEQ * (c % 2) + P * m
                    ins = pe.transpose(bank[2 + c // 2][:, at:at + P], y_attn[m][:, P * c:P * (c + 1)], ident[:, :])
                if c % 2 == 1:
                    ins.then_inc(aT, 1)

            def transpose_f(m):
                pe.wait_ge(f_normed, 2 * m + 2)
                for kc in range(KC):
                    ins = pe.transpose(f_at(kc)[:, P * m:P * (m + 1)], x_norm[m][:, P * kc:P * (kc + 1)], ident[:, :])
                    if m == TT - 1 and kc % 2 == 1:
                        ins.then_inc(fT, 1)

            for m in range(TT):
                for j in range(LC, KC):
                    u = U_O + j
                    split(u)
                    if m == 0:
                        pe.wait_ge(mix_ready, 1 + j - LC + 1)
                    first, second = out_unit(u, m)
                    if j == KC - 1:
                        first.then_inc(wout_done, 1)
                    if m == 0 and j == KC - 1:
                        second.then_inc(wout_done, 1)
                    elif m == 1:
                        second.then_inc(unit_used, 1)
                    if m == 1 and j == KC - 2:
                        transpose_f(0)
            transpose_f(1)

            def ffn_up(s, it=None):
                for which, u in enumerate(ffn_units(s)[0:2]):
                    if s >= 2:
                        pe.wait_ge((conv_g_done, conv_v_done)[which], at_pass(it, LOOP_STEPS, s - 1))
                    cols_unit(u, up_bank(s, which)[:, 0:SEQ], fT_lo if s == 0 and which == 0 else None, it)

            def ffn_down(s, u, it=None):
                split(u, it)
                pe.wait_ge(act_ready, at_pass(it, LOOP_STEPS, s + 1))
                for m in range(TT):
                    ends = down_like(u, [bank[b] for b in DOWN], m, act_hi[:, s % 2, :], act_lo[:, s % 2, :],
                                     s == 0, s == STEPS - 1)
                    if s == STEPS - 1:
                        for end in ends:
                            end.then_inc(down_done, 1)
                if s < STEPS - 1:
                    ends[-1].then_inc(unit_used, 1)

            ffn_up(0)
            for t in range(1, 2):
                ffn_up(t)
                ffn_down(t - 1, ffn_units(t)[2])
            with pe.Fori(0, LOOPS) as it:
                for t in range(2, 2 + LOOP_STEPS):
                    ffn_up(t, it)
                    ffn_down(t - 1, ffn_units(t)[2], it)
            ffn_down(STEPS - 1, U_LAST)


def lay_out(v, np):
    def by_channels(w, col, width, n):
        part = w[:, col:col + width].reshape(KC, P, n, P)
        return part.transpose(2, 1, 0, 3).reshape(n, P, UNIT)

    def by_rows(w, n):
        per = UNIT // w.shape[1]
        return w.reshape(n, per, P, w.shape[1]).transpose(0, 2, 1, 3).reshape(n, P, UNIT)

    w_in, w_up = v["w_in"][0], v["w_up"][0]
    gate_units = by_channels(w_up, 0, D_FF, STEPS)
    value_units = by_channels(w_up, D_FF, D_FF, STEPS)
    down_units = by_rows(v["w_down"][0], STEPS)
    ffn = [gate_units[0], value_units[0]]
    for s in range(1, STEPS):
        ffn += [gate_units[s], value_units[s], down_units[s - 1]]
    ffn.append(down_units[STEPS - 1])
    units = np.concatenate([
        by_channels(w_in, 0, LRU_WIDTH, LC),
        by_rows(w_in[:, 1024:1536], 4),
        by_rows(w_in[:, 1536:2048], 4),
        by_channels(w_in, LRU_WIDTH, LRU_WIDTH, LC),
        by_rows(w_in[:, 2048:2560], 4),
        by_rows(v["w_out"][0], KC),
        np.stack(ffn)])
    stream = units.reshape(DMAS, 2, P, UNIT).transpose(0, 2, 1, 3).reshape(DMAS, P, 2 * UNIT)

    rows = [v["mix_norm_g"], v["lru_conv_w"], v["lru_conv_b"], v["lru_b_a"], v["lru_b_i"], v["lru_lambda"],
            v["lru_out_g"], v["attn_out_g"], v["ffn_norm_g"], v["q_norm_g"], v["q_norm_g"], v["k_norm_g"],
            v["k_norm_g"], v["ffn_conv_w"], v["ffn_conv_b"]]
    params = np.concatenate([r.reshape(-1) for r in rows]).reshape(N_PAR, P).T

    gates = np.zeros((2, LC, P, P), v["lru_w_a"].dtype)
    for g, w in enumerate((v["lru_w_a"][0], v["lru_w_i"][0])):
        for h in range(LRU_HEADS):
            at = LRU_HEAD_DIM * (h % 2)
            gates[g, h // 2, at:at + LRU_HEAD_DIM, at:at + LRU_HEAD_DIM] = w[h]
    gates = gates.transpose(2, 0, 1, 3).reshape(P, 2 * LC * P)
    return {"x": v["x"], "stream": stream, "params": params, "gates": gates}


def kernel(**inputs):
    import numpy as _np
    import concourse.bacc as _bacc
    from concourse import mybir as _mybir
    from concourse.bass_utils import run_bass_kernel_spmd as _run

    nc = _bacc.Bacc("TRN2", target_bir_lowering=False, num_devices=1)
    arrays, args = {}, []
    for name, a in lay_out({k: _np.asarray(a) for k, a in inputs.items()}, _np).items():
        a = _np.ascontiguousarray(a)
        arrays[f"in_{name}_dram"] = a
        args.append(nc.dram_tensor(f"in_{name}_dram", a.shape, _mybir.dt.from_np(a.dtype), kind="ExternalInput").ap())
    args.append(nc.dram_tensor("out_0_dram", (1, SEQ, D_MODEL), _mybir.dt.float32, kind="ExternalOutput").ap())
    build_layer(nc, *args)
    r = _run(nc, [arrays], core_ids=[0])
    return r.results[0]["out_0_dram"]
```

```python
from contextlib import ExitStack

import concourse.bass as bass
from concourse import mybir

F32 = mybir.dt.float32
F32R = mybir.dt.float32r
ACT = mybir.ActivationFunctionType
ALU = mybir.AluOpType
AX_X = mybir.AxisListType.X

P = 128
D_MODEL = 1024
SEQ = 256
LRU_WIDTH = 512
LRU_HEADS = 8
LRU_HEAD_DIM = LRU_WIDTH // LRU_HEADS
LRU_CONV = 4
LRU_C = 8.0
ATTN_WIDTH = 512
HEADS = 8
HEAD_DIM = ATTN_WIDTH // HEADS
D_FF = 2816
FFN_CONV = 3
EPS = 1e-6

KC = D_MODEL // P
TT = SEQ // P
LC = LRU_WIDTH // P
STEPS = D_FF // P
UNIT = 1024
RAW = 6
RING = 6
WARM_UP = 14
F_CUT = 384
P_SLOTS = 5
MASKED = -3.0e38
KEYS = [P, 2 * P]
KEY_AT = [0, P]
SCORES = sum(KEYS)

U_Q, U_K, U_X, U_Y, U_V, U_O = 0, 4, 8, 12, 16, 20
VECTOR_HI = range(17, 23)
U_FFN = 28
LOOP_STEPS = 4
LOOPS = (STEPS - 2) // LOOP_STEPS
LOOP_UNITS = 3 * LOOP_STEPS
U_LOOP = U_FFN + 5
U_LAST = U_LOOP + LOOPS * LOOP_UNITS
UNITS = U_LAST + 1
DMAS = UNITS // 2
assert (STEPS - 2) % LOOP_STEPS == 0 and LOOP_UNITS % RING == 0 and LOOP_UNITS == 2 * RAW and UNITS % 2 == 0

MIX_G, CONV_W, CONV_B, B_A, B_I, LAMBDA = 0, 8, 24, 28, 32, 36
LRU_G, ATTN_G, FFN_G, Q_G, K_G = 40, 44, 48, 56, 57
FFN_W, FFN_B = 58, 58 + FFN_CONV * 2 * STEPS
N_PAR = FFN_B + 2 * STEPS


def build_layer(nc, x, stream, params, gates, out):
    with ExitStack() as ctx:
        def sb(name, shape, dt=F32):
            return ctx.enter_context(nc.sbuf_tensor(name, shape, dt))

        def sem(name):
            return ctx.enter_context(nc.semaphore(name))

        bank = [ctx.enter_context(nc.psum_tensor(f"bank{b}", [P, 512], F32)) for b in range(8)]
        raw = [sb(f"raw{r}", [P, 2 * UNIT]) for r in range(RAW)]
        w_hi = [sb(f"w_hi{r}", [P, UNIT], F32R) for r in range(RING)]
        w_lo = [sb(f"w_lo{r}", [P, UNIT], F32R) for r in range(RING)]
        x_tok = sb("x_tok", [P, TT, D_MODEL])
        h_hi = sb("h_hi", [P, KC, SEQ], F32R)
        h_lo = sb("h_lo", [P, KC, SEQ], F32R)
        mix_hi = sb("mix_hi", [P, KC, SEQ], F32R)
        mix_lo = sb("mix_lo", [P, KC, SEQ], F32R)
        xc = sb("xc", [P, LC, SEQ])
        gate_r = sb("gate_r", [P, LC, SEQ])
        gate_i = sb("gate_i", [P, LC, SEQ])
        decay = sb("decay", [P, LC, SEQ])
        tanh_a = sb("tanh_a", [P, LC, SEQ])
        ygate = sb("ygate", [P, LC, SEQ])
        qk_tok = sb("qk_tok", [P, 2 * TT, ATTN_WIDTH])
        q_T = sb("q_T", [P, LC, SEQ])
        k_T = sb("k_T", [P, LC, SEQ])
        v_tok = sb("v_tok", [P, TT, ATTN_WIDTH])
        p_T = sb("p_T", [P, HEADS, SCORES])
        act_hi = sb("act_hi", [P, 2, SEQ], F32R)
        act_lo = sb("act_lo", [P, 2, SEQ], F32R)
        neg_dist = sb("neg_dist", [P, SCORES])
        ident = sb("ident", [P, P])
        ones = sb("ones", [P, P])
        diag = sb("diag", [P, TT, P])
        par = sb("par", [P, N_PAR])
        small = sb("small", [P, 208])
        probs = [qk_tok[:, :, :].rearrange("p a b -> p (a b)")[:, SCORES * j:SCORES * (j + 1)]
                 for j in range(P_SLOTS)]
        conv_g = [xc[:, j, :] for j in range(2)]
        conv_v = [xc[:, 2 + j, :] for j in range(2)]
        gelu_g = [gate_r[:, j, :] for j in range(2)]
        prod = [gate_i[:, j, :] for j in range(2)]
        y_attn = [q_T[:, :, :].rearrange("p c t -> p (c t)")[:, 0:512],
                  q_T[:, :, :].rearrange("p c t -> p (c t)")[:, 512:1024]]
        w_gate = p_T[:, 4:8, :].rearrange("p h s -> p (h s)")[:, 0:2 * LC * P].rearrange(
            "p (g c j) -> p g c j", g=2, c=LC)

        def flat(t):
            return t[:, :, :].rearrange("p c t -> p (c t)")

        x_norm = [flat(decay), flat(gate_i)]
        sq_tok = flat(p_T)[:, 2560:3072]
        y_sq_sum = gate_r[:, 0, :]
        eps = small[:, 0:1]
        x_ss, x_rms, x_rstd = small[:, 2:4], small[:, 4:6], small[:, 6:8]
        lam_u, lam_z, lam_z2, lam_s, log_c = (small[:, 8 + 4 * j:12 + 4 * j] for j in range(5))
        row_sum = small[:, 28:44].rearrange("p (h m) -> p h m", m=TT)
        neg_max = small[:, 44:60].rearrange("p (h m) -> p h m", m=TT)
        row_rec = small[:, 60:76].rearrange("p (h m) -> p h m", m=TT)
        q_scale = small[:, 76:80]
        y_rms, y_rstd = small[:, 80:82], small[:, 82:84]
        a_ss, a_rms, a_rstd = small[:, 84:86], small[:, 86:88], small[:, 88:90]
        f_ss, f_sum, f_rms, f_rstd = small[:, 200:205], small[:, 94:96], small[:, 96:98], small[:, 98:100]
        lam_p = small[:, 100:104]
        x_part, x_mean = small[:, 206:207], small[:, 207:208]
        warm_out = small[:, 1:2]
        qk_ss, qk_rms, qk_rstd = (small[:, 104 + 32 * j:136 + 32 * j].rearrange("p (g h) -> p g h", h=HEADS)
                                  for j in range(3))

        raw_landed = [sem(f"raw_landed{r}") for r in range(RAW)]
        x_landed = [sem(f"x_landed{m}") for m in range(TT)]
        par_landed, first_landed = sem("par_landed"), sem("first_landed")
        gates_landed = sem("gates_landed")
        out_stored = sem("out_stored")
        hi_done, own_hi, lo_done, unit_used = sem("hi_done"), sem("own_hi"), sem("lo_done"), sem("unit_used")
        first_hi, first_lo = sem("first_hi"), sem("first_lo")
        ones_done, consts, dist_done, q_scale_done = (
            sem("ones_done"), sem("consts"), sem("dist_done"), sem("q_scale_done"))
        x_sq, x_sq_1, x_rms_done, x_rec = sem("x_sq"), sem("x_sq_1"), sem("x_rms_done"), sem("x_rec")
        x_normed = [sem(f"x_normed{m}") for m in range(TT)]
        xT, hT_hi, hT_lo = sem("xT"), sem("hT_hi"), sem("hT_lo")
        qk_sq, qk_sum, qk_rms_done, qk_norm = sem("qk_sq"), sem("qk_sum"), sem("qk_rms_done"), sem("qk_norm")
        qkT, qkT_read = sem("qkT"), sem("qkT_read")
        conv_base, conv_done = sem("conv_base"), sem("conv_done")
        gates_done, gates_read = sem("gates_done"), sem("gates_read")
        lam_exp, log_c_done = sem("lam_exp"), sem("log_c_done")
        decay_done, a2_done, one_m_a2, root_done = sem("decay_done"), sem("a2_done"), sem("one_m_a2"), sem("root_done")
        lru_in, scan_done = sem("lru_in"), sem("scan_done")
        ygate_done, y_done, y_sq, y_chunks = sem("ygate_done"), sem("y_done"), sem("y_sq"), sem("y_chunks")
        y_sum, y_rms_done, y_diag, y_bc = sem("y_sum"), sem("y_rms_done"), sem("y_diag"), sem("y_bc")
        scores, shifted, probs_done = sem("scores"), sem("shifted"), sem("probs_done")
        pT, pT_read = sem("pT"), sem("pT_read")
        v_half, v_ready = sem("v_half"), sem("v_ready")
        o_done, attn_out, a_sq, a_rms_done, a_normed = (
            sem("o_done"), sem("attn_out"), sem("a_sq"), sem("a_rms_done"), sem("a_normed"))
        aT, aT_hi = sem("aT"), sem("aT_hi")
        mix_ready = sem("mix_ready")
        wout_done, x2_done, f_sq, f_added, f_rms_done, f_rec, f_normed = (
            sem("wout_done"), sem("x2_done"), sem("f_sq"), sem("f_added"), sem("f_rms_done"), sem("f_rec"),
            sem("f_normed"))
        fT, fT_hi, fT_lo = sem("fT"), sem("fT_hi"), sem("fT_lo")
        up_base, tap_g, tap_v, conv_g_done, conv_v_done = (
            sem("up_base"), sem("tap_g"), sem("tap_v"), sem("conv_g_done"), sem("conv_v_done"))
        gelu_done, prod_done, act_hi_done, act_ready = (
            sem("gelu_done"), sem("prod_done"), sem("act_hi_done"), sem("act_ready"))
        down_done, final = sem("down_done"), sem("final")
        chain, pool_chain, warm = sem("chain"), sem("pool_chain"), sem("warm")

        def raw_unit(u):
            return raw[(u // 2) % RAW][:, UNIT * (u % 2):UNIT * (u % 2 + 1)]

        def by_chunk(tile):
            return tile[:, :].rearrange("p (kc n) -> p kc n", kc=KC)

        def ffn_units(s):
            if s == 0:
                return [U_FFN, U_FFN + 1]
            return [U_FFN + 3 * s - 1 + k for k in range(3)]

        def up_bank(s, which):
            return bank[(0, 1, 6, 7)[2 * (s % 2) + which]]

        Q_ACC, K_ACC, X_ACC = bank[0:2], bank[2:4], bank[4:8]
        Y_ACC, V_ACC = bank[2:4], bank[4:6]
        QK_T = bank[0:4]
        S_BANK, P_BANK = bank[0:2], bank[6:8]
        Y_NORM, O_BANK, A_T = bank[5], (bank[4], bank[2]), bank[4:6]
        O_PIECES = ((0, slice(0, 512), bank[0][:, 0:512]), (0, slice(512, 1024), bank[1][:, 0:512]),
                    (1, slice(0, 512), bank[6][:, 0:512]), (1, slice(512, 768), bank[7][:, 0:256]),
                    (1, slice(768, 1024), bank[3][:, 0:256]))
        DOWN = (bank[4], bank[5], bank[2], bank[3])

        def hi_count(u):
            return u + 1 - sum(v <= u for v in VECTOR_HI)

        def x_at(kc):
            return bank[2 + kc][:, 0:SEQ] if kc < 4 else bank[6 + (kc - 4) // 2][:, SEQ * (kc % 2):SEQ * (kc % 2 + 1)]

        def f_at(m, kc):
            if m == 0:
                tile, at = bank[4 + kc // 4], kc % 4
            else:
                tile, at = (bank[2], bank[4], bank[5], bank[6])[kc % 4], kc // 4
            return tile[:, P * at:P * (at + 1)]

        def slope(h):
            return 2.0 ** (-8.0 * (h + 1) / HEADS)

        def at_pass(it, per, value):
            return value if it is None else it * per + value

        block = ctx.enter_context(nc.Block())

        @block.sync
        def _(sp):
            x_t = x[0].rearrange("(m p) d -> m p d", p=P)
            for m in range(TT):
                sp.dma_start(x_tok[:, m, :], x_t[m]).then_inc(x_landed[m], 16)

            sp.dma_start(raw[0][:, 0:UNIT], stream[0, :, 0:UNIT]).then_inc(first_landed, 16)
            sp.dma_start(raw[0][:, UNIT:2 * UNIT], stream[0, :, UNIT:2 * UNIT]).then_inc(raw_landed[0], 16)
            for n in range(1, RAW):
                sp.dma_start(raw[n][:, :], stream[n]).then_inc(raw_landed[n], 16)

            with sp.Fori(0, DMAS // RAW - 1) as it:
                for r in range(RAW):
                    sp.wait_ge(lo_done, it * (2 * RAW) + (2 * r + 2))
                    sp.dma_start(raw[r][:, :], stream[bass.ds(it * RAW + (RAW + r), 1)].rearrange(
                        "one p c -> (one p) c")).then_inc(raw_landed[r], 16)
            for n in range(DMAS - DMAS % RAW, DMAS):
                sp.wait_ge(lo_done, 2 * (n - RAW) + 2)
                sp.dma_start(raw[n % RAW][:, :], stream[n]).then_inc(raw_landed[n % RAW], 16)
            out_t = out[0].rearrange("(m p) d -> m p d", p=P)
            for m in range(TT):
                for n in range(2):
                    sp.wait_ge(final, 2 * m + n + 1)
                    sp.dma_start(out_t[m][:, 512 * n:512 * (n + 1)],
                                 x_tok[:, m, 512 * n:512 * (n + 1)]).then_inc(out_stored, 16)
            sp.wait_ge(out_stored, 16 * 2 * TT)

        @block.gpsimd
        def _(pool):
            pool.memset(ones[:, :], 1.0).then_inc(ones_done, 1)
            pool.memset(eps, EPS).then_inc(consts, 1)
            pool.dma_start(par[:, :], params).then_inc(par_landed, 16)
            pool.wait_ge(ones_done, 1)
            pool.affine_select(out=ident[:, :], in_=ones[:, :], compare_op=ALU.is_equal, fill=0.0, base=0,
                               pattern=[[-1, P]], channel_multiplier=1).then_inc(consts, 1)
            for m in range(TT):
                view = neg_dist[:, KEY_AT[m]:KEY_AT[m] + KEYS[m]]
                pool.iota(view, pattern=[[1, KEYS[m]]], base=-P * m, channel_multiplier=-1,
                          allow_small_or_imprecise_dtypes=True).then_inc(pool_chain, 1)
                pool.wait_ge(pool_chain, 1 + m)
                pool.affine_select(out=view, in_=view, compare_op=ALU.is_ge, fill=MASKED, base=P * m,
                                   pattern=[[-1, KEYS[m]]], channel_multiplier=1).then_inc(dist_done, 1)
            for h in range(HEADS):
                half = HEAD_DIM * (h % 2)
                pool.wait_ge(dist_done, TT + h)
                pool.memset(q_scale[half:half + HEAD_DIM, h // 2:h // 2 + 1],
                            HEAD_DIM ** -0.5 / slope(h)).then_inc(dist_done, 1)

            pool.wait_ge(lo_done, 4)
            pool.dma_start(w_gate.rearrange("p g c j -> p (g c j)"), gates).then_inc(gates_landed, 16)

        @block.scalar
        def _(act):
            def hi(u, it=None):
                act.wait_ge(raw_landed[(u // 2) % RAW], at_pass(it, 16, 16 * (u // 2 // RAW + 1)))
                if u >= RING:
                    act.wait_ge(unit_used, at_pass(it, LOOP_UNITS, u - RING + 1))
                act.activation(w_hi[u % RING][:, :], raw_unit(u), ACT.Copy).then_inc(hi_done, 1)

            def his(*units):
                for u in units:
                    hi(u)

            act.wait_ge(consts, 1)
            act.activation(warm_out, eps, ACT.Sqrt).then_inc(warm, 1)
            act.wait_ge(x_landed[0], 16)
            act.activation(flat(ygate), x_tok[:, 0, :], ACT.Square, accum_out=x_ss[:, 0:1]).then_inc(x_sq, 1)
            def x_root(m):
                act.activation(x_rms[:, m:m + 1], x_ss[:, m:m + 1], ACT.Sqrt, bias=eps,
                               scale=1.0 / D_MODEL).then_inc(x_rms_done, 1)

            def x_scale(m):
                act.wait_ge(x_rec, m + 1)
                act.activation(x_norm[m][:, 0:F_CUT], x_tok[:, m, 0:F_CUT], ACT.Copy,
                               scale=x_rstd[:, m:m + 1]).then_inc(x_normed[m], 1)

            act.wait_ge(x_sq, 1)
            act.activation(x_rms[:, 0:1], x_ss[:, 0:1], ACT.Sqrt, bias=eps, scale=1.0 / D_MODEL).then_inc(x_rms_done, 1)
            act.wait_ge(x_landed[1], 16)
            act.activation(flat(ygate)[:, 0:512], x_tok[:, 1, 512:1024], ACT.Square,
                           accum_out=x_ss[:, 1:2]).then_inc(x_sq, 1)
            x_scale(0)
            act.wait_ge(x_sq, 2)
            act.wait_ge(x_sq_1, 1)
            act.activation(x_rms[:, 1:2], x_ss[:, 1:2], ACT.Sqrt, bias=x_mean,
                           scale=1.0 / D_MODEL).then_inc(x_rms_done, 1)
            x_scale(1)

            def h_part(kc):
                act.wait_ge(xT, min(kc, 4 + (kc - 4) // 2) + 1)
                act.activation(h_hi[:, kc, :], x_at(kc), ACT.Copy,
                               scale=par[:, MIX_G + kc:MIX_G + kc + 1]).then_inc(hT_hi, 1)

            act.wait_ge(par_landed, 16)
            h_part(0)
            act.wait_ge(first_landed, 16)
            act.activation(w_hi[0][:, 512:UNIT], raw[0][:, 512:UNIT], ACT.Copy).then_inc(hi_done, 1)
            h_part(1)
            h_part(2)
            his(1)
            for kc in (3, 4, 5):
                h_part(kc)
            his(2)
            for kc in (6, 7):
                h_part(kc)
            his(3, 4, 5, 6, 7, 8)

            def squares(g, acc, last_unit):
                act.wait_ge(unit_used, last_unit + 1)
                if g >= 1:
                    act.wait_ge(qk_sum, g)
                act.activation(sq_tok, acc[:, :], ACT.Square).then_inc(qk_sq, 1)

            def roots(g):
                act.wait_ge(qk_sum, g + TT)
                act.activation(qk_rms[:, g:g + TT, :], qk_ss[:, g:g + TT, :], ACT.Sqrt, bias=eps,
                               scale=1.0 / HEAD_DIM).then_inc(qk_rms_done, 1)

            def conv_first(c):
                act.wait_ge(unit_used, U_X + c + 1)
                w3 = CONV_W + (LRU_CONV - 1) * LC + c
                act.activation(xc[:, c, :], X_ACC[c][:, 0:SEQ], ACT.Identity, bias=par[:, CONV_B + c:CONV_B + c + 1],
                               scale=par[:, w3:w3 + 1]).then_inc(conv_base, 1)

            def exps(h):
                act.wait_ge(shifted, h + 1)
                for m in range(TT):
                    part = slice(KEY_AT[m], KEY_AT[m] + KEYS[m])
                    act.activation(probs[h % P_SLOTS][:, part], probs[h % P_SLOTS][:, part], ACT.Exp, scale=-1.0,
                                   bias=neg_max[:, h, m:m + 1],
                                   accum_out=row_sum[:, h, m:m + 1]).then_inc(probs_done, 1)

            def p_out(h):
                act.wait_ge(pT, h + 1)
                act.activation(p_T[:, h, :], P_BANK[h % 2][:, 0:SCORES], ACT.Copy).then_inc(pT_read, 1)

            squares(0, Q_ACC[0], U_K - 1)
            squares(1, Q_ACC[1], U_K - 1)
            roots(0)
            his(9, 10, 11)
            squares(2, K_ACC[0], U_X - 1)
            squares(3, K_ACC[1], U_X - 1)
            roots(2)
            his(12, 13)
            conv_first(0)
            conv_first(1)
            act.wait_ge(q_scale_done, 1)
            for c in range(LC):
                act.wait_ge(qkT, c + 1)
                act.activation(q_T[:, c, :], QK_T[c][:, 0:SEQ], ACT.Copy, scale=q_scale[:, c:c + 1])
                act.activation(k_T[:, c, :], QK_T[c][:, SEQ:2 * SEQ], ACT.Copy,
                               scale=par[:, K_G:K_G + 1]).then_inc(qkT_read, 1)
            his(14)
            act.activation(lam_z, par[:, LAMBDA:LAMBDA + LC], ACT.Abs).then_inc(lam_exp, 1)
            conv_first(2)
            act.wait_ge(lam_exp, 1)
            act.activation(lam_u, lam_z, ACT.Exp, scale=-1.0).then_inc(lam_exp, 1)
            exps(0)
            exps(1)
            his(15)
            conv_first(3)
            exps(2)
            exps(3)
            his(16)
            for c in range(LC):
                act.wait_ge(gates_done, c + 1)
                act.activation(gate_r[:, c, :], X_ACC[c][:, 0:SEQ], ACT.Sigmoid,
                               bias=par[:, B_A + c:B_A + c + 1])
                act.activation(gate_i[:, c, :], X_ACC[c][:, SEQ:2 * SEQ], ACT.Sigmoid,
                               bias=par[:, B_I + c:B_I + c + 1]).then_inc(gates_read, 1)
            exps(4)
            act.wait_ge(log_c_done, 1)
            act.wait_ge(gates_read, LC)
            for c in range(LC):
                act.activation(decay[:, c, :], gate_r[:, c, :], ACT.Exp, scale=log_c[:, c:c + 1])
                act.activation(tanh_a[:, c, :], gate_r[:, c, :], ACT.Tanh,
                               scale=log_c[:, c:c + 1]).then_inc(decay_done, 1)
                if c < 2:
                    p_out(c)
            act.wait_ge(decay_done, LC)
            act.activation(flat(gate_r), flat(decay), ACT.Square).then_inc(a2_done, 1)
            exps(5)
            p_out(2)
            p_out(3)
            exps(6)
            exps(7)
            p_out(4)
            p_out(5)
            act.wait_ge(one_m_a2, 1)
            act.activation(flat(tanh_a), flat(tanh_a), ACT.Sqrt, scale=-1.0).then_inc(root_done, 1)
            for j in range(2):
                act.wait_ge(unit_used, U_Y + 2 * j + 2)
                act.activation(ygate[:, 2 * j:2 * j + 2, :], Y_ACC[j][:, :].rearrange("p (c t) -> p c t", c=2),
                               ACT.Gelu_apprx_tanh).then_inc(ygate_done, 1)
            p_out(6)
            p_out(7)
            act.wait_ge(y_done, 1)
            act.activation(flat(xc), flat(ygate), ACT.Square).then_inc(y_sq, 1)
            act.activation(warm_out, eps, ACT.Sqrt).then_inc(warm, 1)
            for m in range(TT):
                if m == 0:
                    act.wait_ge(v_half, 1)
                else:
                    act.wait_ge(unit_used, U_O)
                act.activation(v_tok[:, m, :], V_ACC[m][:, :], ACT.Copy).then_inc(v_ready, 1)
            act.wait_ge(y_sum, 1)
            act.activation(y_rms, Y_NORM[:, 0:TT], ACT.Sqrt, bias=eps, scale=1.0 / LRU_WIDTH).then_inc(y_rms_done, 1)
            his(23, 24, 25)
            for m in range(TT):
                act.wait_ge(attn_out, m + 1)
                act.activation(sq_tok, y_attn[m], ACT.Square, accum_out=a_ss[:, m:m + 1]).then_inc(a_sq, 1)
                act.wait_ge(a_sq, m + 1)
                act.activation(a_rms[:, m:m + 1], a_ss[:, m:m + 1], ACT.Sqrt, bias=eps,
                               scale=1.0 / ATTN_WIDTH).then_inc(a_rms_done, 1)
            his(26, 27)
            for c in range(LC):
                act.wait_ge(aT, c // 2 + 1)
                act.activation(mix_hi[:, LC + c, :], A_T[c // 2][:, SEQ * (c % 2):SEQ * (c % 2 + 1)], ACT.Copy,
                               scale=par[:, ATTN_G + c:ATTN_G + c + 1]).then_inc(aT_hi, 1)
            def f_square(i):
                m, cols, _ = O_PIECES[i]
                act.wait_ge(x2_done, i + 1)
                if i:
                    act.wait_ge(f_sq, i)
                act.activation(sq_tok[:, 0:cols.stop - cols.start], x_tok[:, m, cols], ACT.Square,
                               accum_out=f_ss[:, i:i + 1]).then_inc(f_sq, 1)

            def f_norm(m):
                last = (1, len(O_PIECES) - 1)[m]
                act.wait_ge(f_added, (1, 3)[m])
                act.wait_ge(f_sq, last + 1)
                act.activation(f_rms[:, m:m + 1], f_ss[:, last:last + 1], ACT.Sqrt, bias=f_sum[:, m:m + 1],
                               scale=1.0 / D_MODEL).then_inc(f_rms_done, 1)
                act.wait_ge(f_rec, m + 1)
                act.activation(x_norm[m][:, 0:F_CUT], x_tok[:, m, 0:F_CUT], ACT.Copy,
                               scale=f_rstd[:, m:m + 1]).then_inc(f_normed, 1)

            def f_part(m, kc):
                tok = slice(P * m, P * (m + 1))
                if m == 0:
                    act.wait_ge(fT, kc // 4 + 1)
                else:
                    act.wait_ge(fT, 2 + kc % 4 + 1)
                    if kc >= 4:
                        act.wait_ge(fT_lo, KC + kc - 4 + 1)
                act.activation(h_hi[:, kc, tok], f_at(m, kc), ACT.Copy,
                               scale=par[:, FFN_G + kc:FFN_G + kc + 1]).then_inc(fT_hi, 1)

            his(U_FFN, U_FFN + 1)
            f_square(0)
            f_square(1)
            f_norm(0)
            f_square(2)
            for kc in range(KC):
                f_part(0, kc)
            f_square(3)
            f_square(4)
            f_norm(1)
            for kc in range(KC):
                f_part(1, kc)

            def ffn_base(s, which, it=None):
                u = ffn_units(s)[which]
                act.wait_ge(unit_used, at_pass(it, LOOP_UNITS, u + 1))
                col = at_pass(it, LOOP_STEPS, s + which * STEPS)
                act.activation((conv_g, conv_v)[which][s % 2], up_bank(s, which)[:, 0:SEQ], ACT.Identity,
                               bias=par[:, bass.ds(col + FFN_B, 1)],
                               scale=par[:, bass.ds(col + (FFN_W + 4 * STEPS), 1)]).then_inc(up_base, 1)

            def ffn_gelu(s, it=None):
                act.wait_ge(conv_g_done, at_pass(it, LOOP_STEPS, s + 1))
                act.activation(gelu_g[s % 2], conv_g[s % 2], ACT.Gelu_apprx_tanh).then_inc(gelu_done, 1)

            def ffn_step(t, it=None):
                g, v, down = ffn_units(t)
                hi(g, it)
                ffn_base(t - 1, 0, it)
                hi(v, it)
                ffn_base(t - 1, 1, it)
                hi(down, it)
                ffn_gelu(t - 1, it)

            ffn_step(1)
            with act.Fori(0, LOOPS) as it:
                for t in range(2, 2 + LOOP_STEPS):
                    ffn_step(t, it)
            hi(U_LAST)
            ffn_base(STEPS - 1, 0)
            ffn_base(STEPS - 1, 1)
            ffn_gelu(STEPS - 1)

        @block.vector
        def _(dve):
            links = [0]

            def link(ins):
                links[0] += 1
                ins.then_inc(chain, 1)
                dve.wait_ge(chain, links[0])

            def lo(u, it=None):
                if u in VECTOR_HI:
                    dve.wait_ge(raw_landed[(u // 2) % RAW], 16 * (u // 2 // RAW + 1))
                    dve.wait_ge(unit_used, u - RING + 1)
                    dve.tensor_copy(w_hi[u % RING][:, :], raw_unit(u)).then_inc(own_hi, 1)
                    dve.wait_ge(own_hi, u - VECTOR_HI[0] + 1)
                else:
                    dve.wait_ge(hi_done, at_pass(it, LOOP_UNITS, hi_count(u)))
                dve.tensor_tensor(w_lo[u % RING][:, :], raw_unit(u), w_hi[u % RING][:, :].bitcast(F32),
                                  ALU.subtract).then_inc(lo_done, 1)

            def los(*units):
                for u in units:
                    lo(u)

            def make_diag(rms, rstd, m, done):
                link(dve.reciprocal(rstd[:, m:m + 1], rms[:, m:m + 1]))
                dve.tensor_scalar(diag[:, m, :], ident[:, :], rstd[:, m:m + 1], None, ALU.mult).then_inc(done, 1)

            def x_reciprocal(m):
                dve.wait_ge(x_rms_done, m + 1)
                dve.reciprocal(x_rstd[:, m:m + 1], x_rms[:, m:m + 1]).then_inc(x_rec, 1)

            def x_scale(m):
                dve.wait_ge(x_rec, m + 1)
                dve.tensor_scalar(x_norm[m][:, F_CUT:D_MODEL], x_tok[:, m, F_CUT:D_MODEL], x_rstd[:, m:m + 1], None,
                                  ALU.mult).then_inc(x_normed[m], 1)

            x_reciprocal(0)
            dve.wait_ge(x_landed[1], 16)
            half = x_tok[:, 1, 0:512]
            link(dve.tensor_tensor_reduce(flat(tanh_a)[:, 0:512], half, half, 1.0, 0.0, ALU.mult, ALU.add, x_part))
            dve.tensor_scalar(x_mean, x_part, 1.0 / D_MODEL, EPS, ALU.mult, ALU.add).then_inc(x_sq_1, 1)
            x_scale(0)
            x_reciprocal(1)
            x_scale(1)

            def h_part(kc):
                dve.wait_ge(hT_hi, kc + 1 if kc < 4 else kc + 2 - kc % 2)
                dve.scalar_tensor_tensor(h_lo[:, kc, :], x_at(kc), par[:, MIX_G + kc:MIX_G + kc + 1],
                                         h_hi[:, kc, :].bitcast(F32), ALU.mult, ALU.subtract).then_inc(hT_lo, 1)

            def first_half(cols, wait_for, done):
                dve.wait_ge(wait_for, 1)
                dve.tensor_tensor(w_lo[0][:, cols], raw[0][:, cols], w_hi[0][:, cols].bitcast(F32),
                                  ALU.subtract).then_inc(done, 1)

            dve.wait_ge(first_landed, 16)
            dve.tensor_copy(w_hi[0][:, 0:512], raw[0][:, 0:512]).then_inc(first_hi, 1)
            first_half(slice(0, 512), first_hi, first_lo)
            h_part(0)
            first_half(slice(512, UNIT), hi_done, lo_done)
            h_part(1)
            h_part(2)
            los(1)
            for kc in (3, 4, 5):
                h_part(kc)
            los(2)
            for kc in (6, 7):
                h_part(kc)
            los(3)
            dve.wait_ge(dist_done, TT + HEADS)
            dve.tensor_scalar(q_scale, q_scale, par[:, Q_G:Q_G + 1], None, ALU.mult).then_inc(q_scale_done, 1)
            los(4, 5, 6, 7, 8)

            def head_sums(g):
                dve.wait_ge(qk_sq, g + 1)
                dve.tensor_reduce(qk_ss[:, g, :], sq_tok.rearrange("p (h d) -> p h d", h=HEADS), AX_X,
                                  ALU.add).then_inc(qk_sum, 1)

            def head_norms(g, acc):
                dve.wait_ge(qk_rms_done, g // TT + 1)
                link(dve.reciprocal(qk_rstd[:, g:g + TT, :], qk_rms[:, g:g + TT, :]))
                for m in range(TT):
                    dve.tensor_tensor(qk_tok[:, g + m, :].rearrange("p (h d) -> p h d", h=HEADS),
                                      acc[m][:, :].rearrange("p (h d) -> p h d", h=HEADS),
                                      qk_rstd[:, g + m, :].unsqueeze(2).to_broadcast([P, HEADS, HEAD_DIM]),
                                      ALU.mult).then_inc(qk_norm, 1)

            def conv_rest(c):
                dve.wait_ge(conv_base, c + 1)
                for back in range(1, LRU_CONV):
                    col = CONV_W + (LRU_CONV - 1 - back) * LC + c
                    tap = dve.scalar_tensor_tensor(xc[:, c, back:SEQ], X_ACC[c][:, 0:SEQ - back],
                                                   par[:, col:col + 1], xc[:, c, back:SEQ], ALU.mult, ALU.add)
                    if back < LRU_CONV - 1:
                        link(tap)
                tap.then_inc(conv_done, 1)

            def shift(h):
                dve.wait_ge(scores, h + 1)
                if h == 0:
                    dve.wait_ge(dist_done, TT)
                if h >= P_SLOTS:
                    dve.wait_ge(pT, h - P_SLOTS + 1)
                for m in range(TT):
                    part = slice(KEY_AT[m], KEY_AT[m] + KEYS[m])
                    ins = dve.tensor_tensor_reduce(probs[h % P_SLOTS][:, part], S_BANK[h % 2][:, part],
                                                   neg_dist[:, part], -slope(h), 3.4e38, ALU.add, ALU.min,
                                                   neg_max[:, h, m:m + 1])
                ins.then_inc(shifted, 1)

            head_sums(0)
            head_sums(1)
            head_norms(0, Q_ACC)
            los(9, 10, 11)
            head_sums(2)
            head_sums(3)
            head_norms(2, K_ACC)
            los(12, 13)
            conv_rest(0)
            conv_rest(1)
            los(14)
            shift(0)
            shift(1)
            conv_rest(2)
            los(15)
            shift(2)
            shift(3)
            conv_rest(3)
            los(16)
            dve.wait_ge(lam_exp, 2)
            link(dve.tensor_scalar(lam_z, lam_u, 2.0, None, ALU.add))
            link(dve.reciprocal(lam_z2, lam_z))
            link(dve.tensor_tensor(lam_z, lam_u, lam_z2, ALU.mult))
            link(dve.tensor_tensor(lam_z2, lam_z, lam_z, ALU.mult))
            link(dve.tensor_scalar(lam_s, lam_z2, 1.0 / 17, None, ALU.mult))
            for k in range(7, 0, -1):
                link(dve.scalar_tensor_tensor(lam_s, lam_s, 1.0 / (2 * k + 1), lam_z2, ALU.add, ALU.mult))
            link(dve.scalar_tensor_tensor(lam_s, lam_s, 1.0, lam_z, ALU.add, ALU.mult))
            link(dve.tensor_scalar(lam_p, par[:, LAMBDA:LAMBDA + LC], -1.0, 0.0, ALU.mult, ALU.max))
            link(dve.scalar_tensor_tensor(lam_p, lam_s, 2.0, lam_p, ALU.mult, ALU.add))
            dve.tensor_scalar(log_c, lam_p, -LRU_C, None, ALU.mult).then_inc(log_c_done, 1)
            shift(4)
            dve.wait_ge(gates_read, LC)
            dve.wait_ge(conv_done, LC)
            dve.tensor_tensor(flat(gate_i), flat(gate_i), flat(xc), ALU.mult).then_inc(lru_in, 1)
            shift(5)
            los(17, 18)
            dve.wait_ge(a2_done, 1)
            dve.scalar_tensor_tensor(flat(tanh_a), flat(gate_r), 1.0, flat(tanh_a), ALU.add,
                                     ALU.mult).then_inc(one_m_a2, 1)
            shift(6)
            shift(7)
            los(19, 20)
            dve.wait_ge(root_done, 1)
            dve.wait_ge(lru_in, 1)
            link(dve.tensor_tensor(flat(gate_r), flat(tanh_a), flat(gate_i), ALU.mult))
            for c in range(LC):
                dve.tensor_tensor_scan(tanh_a[:, c, :], decay[:, c, :], gate_r[:, c, :], 0.0, ALU.mult,
                                       ALU.add).then_inc(scan_done, 1)
            dve.wait_ge(ygate_done, 2)
            dve.wait_ge(scan_done, LC)
            dve.tensor_tensor(flat(ygate), flat(tanh_a), flat(ygate), ALU.mult).then_inc(y_done, 1)
            los(21)
            dve.wait_ge(y_sq, 1)
            dve.tensor_reduce(y_sq_sum, xc[:, :, :].rearrange("p c t -> p t c"), AX_X, ALU.add).then_inc(y_chunks, 1)
            los(22)
            dve.wait_ge(consts, 2)
            dve.wait_ge(y_rms_done, 1)
            for m in range(TT):
                make_diag(y_rms, y_rstd, m, y_diag)
            dve.wait_ge(y_bc, 1)

            def lru_norm(c):
                link(dve.scalar_tensor_tensor(decay[:, c, :], ygate[:, c, :], par[:, LRU_G + c:LRU_G + c + 1],
                                              Y_NORM[:, SEQ:2 * SEQ], ALU.mult, ALU.mult))
                link(dve.tensor_copy(mix_hi[:, c, :], decay[:, c, :]))
                dve.tensor_tensor(mix_lo[:, c, :], decay[:, c, :], mix_hi[:, c, :].bitcast(F32),
                                  ALU.subtract).then_inc(mix_ready, 1)

            lru_norm(0)
            lru_norm(1)
            dve.wait_ge(probs_done, HEADS * TT)
            link(dve.reciprocal(row_rec, row_sum))
            dve.wait_ge(o_done, 1)
            for m in range(TT):
                dve.tensor_tensor(y_attn[m].rearrange("p (h d) -> p h d", h=HEADS),
                                  O_BANK[m][:, :].rearrange("p (h d) -> p h d", h=HEADS),
                                  row_rec[:, :, m:m + 1].to_broadcast([P, HEADS, HEAD_DIM]),
                                  ALU.mult).then_inc(attn_out, 1)
            lru_norm(2)
            los(23)
            for m in range(TT):
                dve.wait_ge(a_rms_done, m + 1)
                link(dve.reciprocal(a_rstd[:, m:m + 1], a_rms[:, m:m + 1]))
                dve.tensor_scalar(y_attn[m], y_attn[m], a_rstd[:, m:m + 1], None, ALU.mult).then_inc(a_normed, 1)
            lru_norm(3)
            los(24, 25)
            for j in range(2):
                dve.wait_ge(aT_hi, 2 * j + 2)
                for c in (2 * j, 2 * j + 1):
                    dve.scalar_tensor_tensor(mix_lo[:, LC + c, :], A_T[j][:, SEQ * (c % 2):SEQ * (c % 2 + 1)],
                                             par[:, ATTN_G + c:ATTN_G + c + 1],
                                             mix_hi[:, LC + c, :].bitcast(F32),
                                             ALU.mult, ALU.subtract).then_inc(mix_ready, 1)
            los(26, 27)
            def f_add(i):
                m, cols, acc = O_PIECES[i]
                if i == len(O_PIECES) - 1:
                    dve.wait_ge(unit_used, U_FFN)
                else:
                    dve.wait_ge(wout_done, i + 1)
                dve.tensor_tensor(x_tok[:, m, cols], x_tok[:, m, cols], acc, ALU.add).then_inc(x2_done, 1)

            def f_mean(i):
                m = O_PIECES[i][0]
                dve.wait_ge(f_sq, i + 1)
                if i in (0, 2):
                    dve.tensor_scalar(f_sum[:, m:m + 1], f_ss[:, i:i + 1], 1.0 / D_MODEL, EPS, ALU.mult,
                                      ALU.add).then_inc(f_added, 1)
                else:
                    dve.wait_ge(f_added, 2)
                    dve.scalar_tensor_tensor(f_sum[:, m:m + 1], f_ss[:, i:i + 1], 1.0 / D_MODEL, f_sum[:, m:m + 1],
                                             ALU.mult, ALU.add).then_inc(f_added, 1)

            def f_norm(m):
                dve.wait_ge(f_rms_done, m + 1)
                dve.reciprocal(f_rstd[:, m:m + 1], f_rms[:, m:m + 1]).then_inc(f_rec, 1)
                dve.wait_ge(f_rec, m + 1)
                dve.tensor_scalar(x_norm[m][:, F_CUT:D_MODEL], x_tok[:, m, F_CUT:D_MODEL], f_rstd[:, m:m + 1], None,
                                  ALU.mult).then_inc(f_normed, 1)

            def f_part(m, kc):
                tok = slice(P * m, P * (m + 1))
                dve.wait_ge(fT_hi, 4 * (kc // 4 + 1) if m == 0 else KC + kc + 1)
                dve.scalar_tensor_tensor(h_lo[:, kc, tok], f_at(m, kc), par[:, FFN_G + kc:FFN_G + kc + 1],
                                         h_hi[:, kc, tok].bitcast(F32), ALU.mult, ALU.subtract).then_inc(fT_lo, 1)

            los(U_FFN, U_FFN + 1)
            f_add(0)
            f_add(1)
            f_mean(0)
            f_norm(0)
            f_add(2)
            f_mean(2)
            for kc in range(KC // 2):
                f_part(0, kc)
            f_add(3)
            f_add(4)
            f_mean(3)
            for kc in range(KC // 2, KC):
                f_part(0, kc)
            f_norm(1)
            for kc in range(KC):
                f_part(1, kc)

            def ffn_taps(s, which, tapped, done, it=None):
                dve.wait_ge(up_base, at_pass(it, 2 * LOOP_STEPS, 2 * s + which + 1))
                acc, col = (conv_g, conv_v)[which][s % 2], at_pass(it, LOOP_STEPS, s + which * STEPS)
                dve.scalar_tensor_tensor(acc[:, 1:SEQ], up_bank(s, which)[:, 0:SEQ - 1],
                                         par[:, bass.ds(col + (FFN_W + 2 * STEPS), 1)], acc[:, 1:SEQ],
                                         ALU.mult, ALU.add).then_inc(tapped, 1)
                dve.wait_ge(tapped, at_pass(it, LOOP_STEPS, s + 1))
                dve.scalar_tensor_tensor(acc[:, 2:SEQ], up_bank(s, which)[:, 0:SEQ - 2],
                                         par[:, bass.ds(col + FFN_W, 1)], acc[:, 2:SEQ],
                                         ALU.mult, ALU.add).then_inc(done, 1)

            def ffn_act(s, it=None):
                count = at_pass(it, LOOP_STEPS, s + 1)
                dve.wait_ge(gelu_done, count)
                dve.wait_ge(conv_v_done, count)
                dve.tensor_tensor(prod[s % 2], gelu_g[s % 2], conv_v[s % 2], ALU.mult).then_inc(prod_done, 1)
                if s >= 1:
                    dve.wait_ge(unit_used, at_pass(it, LOOP_UNITS, U_FFN - 1 + 3 * s))
                dve.wait_ge(prod_done, count)
                dve.tensor_copy(act_hi[:, s % 2, :], prod[s % 2]).then_inc(act_hi_done, 1)
                dve.wait_ge(act_hi_done, count)
                dve.tensor_tensor(act_lo[:, s % 2, :], prod[s % 2], act_hi[:, s % 2, :].bitcast(F32),
                                  ALU.subtract).then_inc(act_ready, 1)

            def ffn_step(t, it=None):
                g, v, down = ffn_units(t)
                lo(g, it)
                ffn_taps(t - 1, 0, tap_g, conv_g_done, it)
                lo(v, it)
                ffn_taps(t - 1, 1, tap_v, conv_v_done, it)
                lo(down, it)
                ffn_act(t - 1, it)

            ffn_step(1)
            with dve.Fori(0, LOOPS) as it:
                for t in range(2, 2 + LOOP_STEPS):
                    ffn_step(t, it)
            lo(U_LAST)
            ffn_taps(STEPS - 1, 0, tap_g, conv_g_done)
            ffn_taps(STEPS - 1, 1, tap_v, conv_v_done)
            ffn_act(STEPS - 1)
            for m in range(TT):
                for n in range(2):
                    half = slice(512 * n, 512 * (n + 1))
                    dve.wait_ge(down_done, 2 * m + n + 1)
                    dve.tensor_tensor(x_tok[:, m, half], x_tok[:, m, half], DOWN[2 * m + n][:, :],
                                      ALU.add).then_inc(final, 1)

        @block.tensor
        def _(pe):
            def three(acc, lhs_hi, lhs_lo, rhs_hi, rhs_lo, first, last, lo_ready=None):
                pe.matmul(acc, lhs_hi, rhs_hi, start=first, stop=False)
                pe.matmul(acc, lhs_hi, rhs_lo, start=False, stop=False)
                if lo_ready is not None:
                    pe.wait_ge(*lo_ready)
                return pe.matmul(acc, lhs_lo, rhs_hi, start=False, stop=last)

            def split(u, it=None):
                pe.wait_ge(lo_done, at_pass(it, LOOP_UNITS, u + 1))

            def cols_unit(u, acc, it=None, h_ready=None):
                split(u, it)
                whi, wlo = by_chunk(w_hi[u % RING]), by_chunk(w_lo[u % RING])
                for kc in range(KC):
                    if h_ready is not None:
                        pe.wait_ge(h_ready, KC + kc + 1)
                    ins = three(acc, whi[:, kc, :], wlo[:, kc, :], h_hi[:, kc, :], h_lo[:, kc, :],
                                kc == 0, kc == KC - 1)
                ins.then_inc(unit_used, 1)

            def rows_unit(u, first_unit, banks, h_ready=None):
                for k in range(2):
                    if u == 0 and k == 0:
                        pe.wait_ge(first_lo, 1)
                    else:
                        split(u)
                    kc, cols = 2 * (u - first_unit) + k, slice(512 * k, 512 * (k + 1))
                    if h_ready is not None:
                        pe.wait_ge(h_ready, kc + 1)
                    for m in range(TT):
                        tok = slice(P * m, P * (m + 1))
                        ins = three(banks[m][:, :], h_hi[:, kc, tok], h_lo[:, kc, tok],
                                    w_hi[u % RING][:, cols], w_lo[u % RING][:, cols], kc == 0, kc == KC - 1)
                ins.then_inc(unit_used, 1)

            def down_like(u, banks, m, n, lhs_hi, lhs_lo, first, last, lo_ready):
                tok = slice(P * m, P * (m + 1))
                return three(banks[2 * m + n][:, :], lhs_hi[:, tok], lhs_lo[:, tok],
                             w_hi[u % RING][:, 512 * n:512 * (n + 1)], w_lo[u % RING][:, 512 * n:512 * (n + 1)],
                             first, last, lo_ready)

            def warm_up(products):
                for _ in range(products):
                    pe.matmul(bank[0][:, 0:P], ones[:, :], ones[:, :], start=True, stop=True)

            pe.wait_ge(ones_done, 1)
            warm_up(WARM_UP)
            pe.wait_ge(consts, 2)
            for m in range(TT):
                pe.wait_ge(x_normed[m], 2)
                for kc in range(KC):
                    ins = pe.transpose(x_at(kc)[:, P * m:P * (m + 1)], x_norm[m][:, P * kc:P * (kc + 1)], ident[:, :])
                    if m == TT - 1 and (kc < 4 or kc % 2 == 1):
                        ins.then_inc(xT, 1)

            def transpose_qk(c):
                for g in range(2 * TT):
                    ins = pe.transpose(QK_T[c][:, P * g:P * (g + 1)], qk_tok[:, g, P * c:P * (c + 1)], ident[:, :])
                ins.then_inc(qkT, 1)

            def score(h):
                c, rows_h = h // 2, slice(HEAD_DIM * (h % 2), HEAD_DIM * (h % 2 + 1))
                if h == 0:
                    pe.wait_ge(qkT_read, LC)
                if h >= 2:
                    pe.wait_ge(shifted, h - 1)
                for m in range(TT):
                    ins = pe.matmul(S_BANK[h % 2][:, KEY_AT[m]:KEY_AT[m] + KEYS[m]],
                                    q_T[rows_h, c, P * m:P * (m + 1)], k_T[rows_h, c, 0:KEYS[m]],
                                    start=True, stop=True)
                ins.then_inc(scores, 1)

            def transpose_p(h):
                pe.wait_ge(probs_done, TT * (h + 1))
                if h == 0:
                    pe.wait_ge(gates_read, LC)
                if h >= 2:
                    pe.wait_ge(pT_read, h - 1)
                for b in range(SCORES // P):
                    ins = pe.transpose(P_BANK[h % 2][:, P * b:P * (b + 1)], probs[h % P_SLOTS][:, P * b:P * (b + 1)],
                                       ident[:, :])
                ins.then_inc(pT, 1)

            def gates_product(c):
                pe.wait_ge(conv_done, c + 1)
                pe.matmul(X_ACC[c][:, 0:SEQ], w_gate[:, 0, c, :], xc[:, c, :], start=True, stop=True)
                pe.matmul(X_ACC[c][:, SEQ:2 * SEQ], w_gate[:, 1, c, :], xc[:, c, :], start=True,
                          stop=True).then_inc(gates_done, 1)

            def y_unit(c):
                cols_unit(U_Y + c, Y_ACC[c // 2][:, SEQ * (c % 2):SEQ * (c % 2 + 1)])

            def head(h):
                return slice(HEAD_DIM * h, HEAD_DIM * (h + 1))

            def y_sums():
                pe.wait_ge(y_chunks, 1)
                for m in range(TT):
                    ins = pe.matmul(Y_NORM[:, m:m + 1], y_sq_sum[:, P * m:P * (m + 1)], ones[:, 0:1],
                                    start=True, stop=True)
                ins.then_inc(y_sum, 1)

            def y_broadcast():
                pe.wait_ge(y_diag, TT)
                for m in range(TT):
                    ins = pe.matmul(Y_NORM[:, SEQ + P * m:SEQ + P * (m + 1)], ones[:, :], diag[:, m, :],
                                    start=True, stop=True)
                ins.then_inc(y_bc, 1)

            def out_piece(u, i):
                kc, (m, cols, acc) = u - U_O, O_PIECES[i]
                tok = slice(P * m, P * (m + 1))
                pe.wait_ge(mix_ready, kc + 1)
                return three(acc, mix_hi[:, kc, tok], mix_lo[:, kc, tok], w_hi[u % RING][:, cols],
                             w_lo[u % RING][:, cols], kc == 0, kc == KC - 1)

            def transpose_a():
                pe.wait_ge(a_normed, TT)
                pe.wait_ge(mix_ready, LC)
                for c in range(LC):
                    for m in range(TT):
                        at = SEQ * (c % 2) + P * m
                        ins = pe.transpose(A_T[c // 2][:, at:at + P], y_attn[m][:, P * c:P * (c + 1)], ident[:, :])
                    if c % 2 == 1:
                        ins.then_inc(aT, 1)

            def transpose_f(m):
                pe.wait_ge(f_normed, 2 * m + 2)
                for group in ((range(0, 4), range(4, 8)), ((0, 4), (1, 5), (2, 6), (3, 7)))[m]:
                    for k in group:
                        ins = pe.transpose(f_at(m, k), x_norm[m][:, P * k:P * (k + 1)], ident[:, :])
                    ins.then_inc(fT, 1)

            for j in range(U_K - U_Q):
                rows_unit(U_Q + j, U_Q, Q_ACC, hT_lo)
            for j in range(U_X - U_K):
                rows_unit(U_K + j, U_K, K_ACC)
            cols_unit(U_X, X_ACC[0][:, 0:SEQ])
            cols_unit(U_X + 1, X_ACC[1][:, 0:SEQ])
            pe.wait_ge(qk_norm, 2 * TT)
            for c in range(LC):
                transpose_qk(c)
            cols_unit(U_X + 2, X_ACC[2][:, 0:SEQ])
            score(0)
            score(1)
            cols_unit(U_X + 3, X_ACC[3][:, 0:SEQ])
            score(2)
            score(3)
            y_unit(0)
            pe.wait_ge(gates_landed, 16)
            for c in range(LC):
                gates_product(c)
            score(4)
            y_unit(1)
            transpose_p(0)
            transpose_p(1)
            score(5)
            y_unit(2)
            transpose_p(2)
            transpose_p(3)
            score(6)
            score(7)
            y_unit(3)
            transpose_p(4)
            transpose_p(5)
            rows_unit(U_V, U_V, V_ACC)
            transpose_p(6)
            transpose_p(7)
            rows_unit(U_V + 1, U_V, V_ACC)
            rows_unit(U_V + 2, U_V, V_ACC)
            split(U_V + 3)
            for m in range(TT):
                for k in range(2):
                    kc, cols, tok = KC - 2 + k, slice(512 * k, 512 * (k + 1)), slice(P * m, P * (m + 1))
                    at = (U_V + 3) % RING
                    ins = three(V_ACC[m][:, :], h_hi[:, kc, tok], h_lo[:, kc, tok],
                                w_hi[at][:, cols], w_lo[at][:, cols], False, k == 1)
                ins.then_inc((v_half, unit_used)[m], 1)
            pe.wait_ge(pT_read, HEADS)
            pe.wait_ge(v_ready, 1)
            for h in range(HEADS):
                pe.matmul(O_BANK[0][:, head(h)], p_T[:, h, 0:P], v_tok[:, 0, head(h)], start=True, stop=True)
            pe.wait_ge(v_ready, TT)
            y_sums()
            for h in range(HEADS):
                if h == HEADS // 2:
                    y_broadcast()
                pe.matmul(O_BANK[1][:, head(h)], p_T[:, h, P:2 * P], v_tok[:, 0, head(h)], start=True, stop=False)
                ins = pe.matmul(O_BANK[1][:, head(h)], p_T[:, h, 2 * P:3 * P], v_tok[:, 1, head(h)],
                                start=False, stop=True)
            ins.then_inc(o_done, 1)

            pe.wait_ge(shifted, HEADS)
            for j in range(LC):
                if j == LC - 1:
                    transpose_a()
                u = U_O + j
                split(u)
                for i in range(len(O_PIECES)):
                    ins = out_piece(u, i)
                ins.then_inc(unit_used, 1)

            for j in range(LC, KC):
                split(U_O + j)
                for i in range(2):
                    ins = out_piece(U_O + j, i)
                    if j == KC - 1:
                        ins.then_inc(wout_done, 1)
            for i in range(2, len(O_PIECES)):
                for j in range(LC, KC):
                    ins = out_piece(U_O + j, i)
                    if i == len(O_PIECES) - 1:
                        ins.then_inc(unit_used, 1)
                if i < len(O_PIECES) - 1:
                    ins.then_inc(wout_done, 1)
                if i == 2:
                    transpose_f(0)
            warm_up(10)
            pe.wait_ge(fT_lo, KC)
            transpose_f(1)

            def ffn_up(s, it=None):
                for which, u in enumerate(ffn_units(s)[0:2]):
                    if s >= 2:
                        pe.wait_ge((conv_g_done, conv_v_done)[which], at_pass(it, LOOP_STEPS, s - 1))
                    cols_unit(u, up_bank(s, which)[:, 0:SEQ], it, fT_lo if s == 0 and which == 0 else None)

            def ffn_down(s, u, it=None):
                split(u, it)
                if s < STEPS - 1:
                    pe.wait_ge(act_ready, at_pass(it, LOOP_STEPS, s + 1))
                else:
                    pe.wait_ge(act_hi_done, s + 1)
                for m in range(TT):
                    for n in range(2):
                        ins = down_like(u, DOWN, m, n, act_hi[:, s % 2, :], act_lo[:, s % 2, :],
                                        s == 0, s == STEPS - 1, (act_ready, STEPS) if s == STEPS - 1 else None)
                        if s == STEPS - 1:
                            ins.then_inc(down_done, 1)
                if s < STEPS - 1:
                    ins.then_inc(unit_used, 1)

            ffn_up(0)
            ffn_up(1)
            ffn_down(0, ffn_units(1)[2])
            with pe.Fori(0, LOOPS) as it:
                for t in range(2, 2 + LOOP_STEPS):
                    ffn_up(t, it)
                    ffn_down(t - 1, ffn_units(t)[2], it)
            ffn_down(STEPS - 1, U_LAST)


def lay_out(v, np):
    def by_channels(w, col, width, n):
        part = w[:, col:col + width].reshape(KC, P, n, P)
        return part.transpose(2, 1, 0, 3).reshape(n, P, UNIT)

    def by_rows(w, n):
        per = UNIT // w.shape[1]
        return w.reshape(n, per, P, w.shape[1]).transpose(0, 2, 1, 3).reshape(n, P, UNIT)

    w_in, w_up = v["w_in"][0], v["w_up"][0]
    gate_units = by_channels(w_up, 0, D_FF, STEPS)
    value_units = by_channels(w_up, D_FF, D_FF, STEPS)
    down_units = by_rows(v["w_down"][0], STEPS)
    ffn = [gate_units[0], value_units[0]]
    for s in range(1, STEPS):
        ffn += [gate_units[s], value_units[s], down_units[s - 1]]
    ffn.append(down_units[STEPS - 1])
    units = np.concatenate([
        by_rows(w_in[:, 1024:1536], 4),
        by_rows(w_in[:, 1536:2048], 4),
        by_channels(w_in, 0, LRU_WIDTH, LC),
        by_channels(w_in, LRU_WIDTH, LRU_WIDTH, LC),
        by_rows(w_in[:, 2048:2560], 4),
        by_rows(v["w_out"][0], KC),
        np.stack(ffn)])
    stream = units.reshape(DMAS, 2, P, UNIT).transpose(0, 2, 1, 3).reshape(DMAS, P, 2 * UNIT)

    rows = [v["mix_norm_g"], v["lru_conv_w"], v["lru_conv_b"], v["lru_b_a"], v["lru_b_i"], v["lru_lambda"],
            v["lru_out_g"], v["attn_out_g"], v["ffn_norm_g"], v["q_norm_g"], v["q_norm_g"], v["k_norm_g"],
            v["k_norm_g"], v["ffn_conv_w"], v["ffn_conv_b"]]
    params = np.concatenate([r.reshape(-1) for r in rows]).reshape(N_PAR, P).T

    gates = np.zeros((2, LC, P, P), v["lru_w_a"].dtype)
    for g, w in enumerate((v["lru_w_a"][0], v["lru_w_i"][0])):
        for h in range(LRU_HEADS):
            at = LRU_HEAD_DIM * (h % 2)
            gates[g, h // 2, at:at + LRU_HEAD_DIM, at:at + LRU_HEAD_DIM] = w[h]
    gates = gates.transpose(2, 0, 1, 3).reshape(P, 2 * LC * P)
    return {"x": v["x"], "stream": stream, "params": params, "gates": gates}


def kernel(**inputs):
    import numpy as _np
    import concourse.bacc as _bacc
    from concourse import mybir as _mybir
    from concourse.bass_utils import run_bass_kernel_spmd as _run

    nc = _bacc.Bacc("TRN2", target_bir_lowering=False, num_devices=1)
    arrays, args = {}, []
    for name, a in lay_out({k: _np.asarray(a) for k, a in inputs.items()}, _np).items():
        a = _np.ascontiguousarray(a)
        arrays[f"in_{name}_dram"] = a
        args.append(nc.dram_tensor(f"in_{name}_dram", a.shape, _mybir.dt.from_np(a.dtype), kind="ExternalInput").ap())
    args.append(nc.dram_tensor("out_0_dram", (1, SEQ, D_MODEL), _mybir.dt.float32, kind="ExternalOutput").ap())
    build_layer(nc, *args)
    r = _run(nc, [arrays], core_ids=[0])
    return r.results[0]["out_0_dram"]
```
